# Optimizing a Trainium2 kernel written in Bass

```python
import math
import jax, jax.numpy as jnp
from jax import lax
import numpy as np

D_MODEL = 1024
BATCH = 1
SEQ = 1024
DEPTH = 1

D_MIX = D_MODEL
LRU_WIDTH = D_MIX // 2
LRU_BLOCKS = 8
LRU_BLOCK = LRU_WIDTH // LRU_BLOCKS
CONV_WIDTH = 4
LRU_C = 8.0
ATT_HEAD_DIM = 64
ATT_WIDTH = D_MIX - LRU_WIDTH
ATT_HEADS = ATT_WIDTH // (2 * ATT_HEAD_DIM)
ATT_V_DIM = 2 * ATT_HEAD_DIM
Q_BLOCK = 128
ROPE_THETA = 10000.0
D_FF = 4 * D_MODEL
NORM_EPS = 1e-6
IN_COLS = 2 * LRU_WIDTH + 3 * ATT_WIDTH

kernel_name = "hymba_style_rglru_diffattn_layer"

def rms_norm(x, g):
    xf = x.astype(jnp.float32)
    y = xf * lax.rsqrt(jnp.mean(xf * xf, axis=-1, keepdims=True) + NORM_EPS)
    return (y * g.astype(jnp.float32)).astype(x.dtype)

def lambda_init(layer_idx):
    return 0.8 - 0.6 * math.exp(-0.3 * layer_idx)

def apply_rope(t, pos):
    half = t.shape[-1] // 2
    freqs = ROPE_THETA ** (-jnp.arange(half, dtype=jnp.float32) / half)
    ang = pos.astype(jnp.float32)[:, None] * freqs[None, :]
    cos = jnp.cos(ang)[None, :, None, None, :]
    sin = jnp.sin(ang)[None, :, None, None, :]
    tf = t.astype(jnp.float32)
    t1, t2 = tf[..., :half], tf[..., half:]
    out = jnp.concatenate([t1 * cos - t2 * sin, t2 * cos + t1 * sin], axis=-1)
    return out.astype(t.dtype)

def rglru_group(u, gate_in, conv_w, conv_b, w_gate_a, b_gate_a, w_gate_x, b_gate_x, lru_lambda):
    B, T, C = u.shape
    xc = lax.conv_general_dilated(
        u, conv_w[:, None, :].astype(u.dtype), window_strides=(1,),
        padding=[(CONV_WIDTH - 1, 0)], dimension_numbers=("NWC", "WIO", "NWC"),
        feature_group_count=C) + conv_b
    xb = xc.reshape(B, T, LRU_BLOCKS, LRU_BLOCK)
    r = jax.nn.sigmoid(jnp.einsum("bthi,hij->bthj", xb, w_gate_a).reshape(B, T, C) + b_gate_a)
    i = jax.nn.sigmoid(jnp.einsum("bthi,hij->bthj", xb, w_gate_x).reshape(B, T, C) + b_gate_x)
    log_a = -LRU_C * r.astype(jnp.float32) * jax.nn.softplus(-lru_lambda.astype(jnp.float32))
    a = jnp.exp(log_a)
    b = jnp.sqrt(-jnp.expm1(2.0 * log_a)) * (i * xc).astype(jnp.float32)

    def combine(e1, e2):
        a1, b1 = e1
        a2, b2 = e2
        return a1 * a2, a2 * b1 + b2

    _, hseq = lax.associative_scan(combine, (a, b), axis=1)
    return hseq.astype(u.dtype) * jax.nn.gelu(gate_in)

def diff_attn_group(q, k, v, lq1, lk1, lq2, lk2, head_gain, lam_init):
    B, T, _ = q.shape
    pos = jnp.arange(T)
    q = apply_rope(q.reshape(B, T, ATT_HEADS, 2, ATT_HEAD_DIM), pos)
    k = apply_rope(k.reshape(B, T, ATT_HEADS, 2, ATT_HEAD_DIM), pos)
    v = v.reshape(B, T, ATT_HEADS, ATT_V_DIM)
    f32 = jnp.float32
    lam = (jnp.exp(jnp.sum(lq1.astype(f32) * lk1.astype(f32)))
           - jnp.exp(jnp.sum(lq2.astype(f32) * lk2.astype(f32))) + lam_init)
    scale = ATT_HEAD_DIM ** -0.5
    nb = T // Q_BLOCK
    qb = q.reshape(B, nb, Q_BLOCK, ATT_HEADS, 2, ATT_HEAD_DIM).transpose(1, 0, 2, 3, 4, 5)
    kpos = jnp.arange(T)

    def one_block(args):
        qblk, bi = args
        s = jnp.einsum("bqhmd,bkhmd->bhmqk", qblk, k).astype(f32) * scale
        qpos = bi * Q_BLOCK + jnp.arange(Q_BLOCK)
        causal = kpos[None, :] <= qpos[:, None]
        s = jnp.where(causal, s, jnp.float32(-1e30))
        p = jax.nn.softmax(s, axis=-1)
        w = p[:, :, 0] - lam * p[:, :, 1]
        return jnp.einsum("bhqk,bkhe->bqhe", w.astype(v.dtype), v)

    o = lax.map(one_block, (qb, jnp.arange(nb)))
    o = o.transpose(1, 0, 2, 3, 4).reshape(B, T, ATT_HEADS, ATT_V_DIM)
    o = rms_norm(o, head_gain) * (1.0 - lam_init)
    return o.reshape(B, T, ATT_WIDTH)

def setup_inputs(seed: int = 0) -> dict:
    key = jax.random.key(seed)
    ks = jax.random.split(key, 24)
    f32 = jnp.float32
    L = DEPTH

    def nrm(k, shape, scale):
        return jax.random.normal(k, shape, f32) * scale

    def gain(k, n):
        return 1.0 + 0.02 * jax.random.normal(k, (L, n), f32)

    u = jax.random.uniform(ks[10], (L, LRU_WIDTH), f32, 0.9, 0.999)
    a0 = u ** (1.0 / LRU_C)
    lru_lambda = jnp.log(a0) - jnp.log1p(-a0)
    return {
        "x": jax.random.normal(ks[0], (BATCH, SEQ, D_MODEL), f32),
        "norm_mix_pre": gain(ks[1], D_MODEL),
        "w_in": nrm(ks[2], (L, D_MODEL, IN_COLS), D_MODEL ** -0.5),
        "conv_w": nrm(ks[3], (L, CONV_WIDTH, LRU_WIDTH), CONV_WIDTH ** -0.5),
        "conv_b": nrm(ks[4], (L, LRU_WIDTH), 0.01),
        "w_gate_a": nrm(ks[5], (L, LRU_BLOCKS, LRU_BLOCK, LRU_BLOCK), LRU_BLOCK ** -0.5),
        "b_gate_a": nrm(ks[6], (L, LRU_WIDTH), 0.01),
        "w_gate_x": nrm(ks[7], (L, LRU_BLOCKS, LRU_BLOCK, LRU_BLOCK), LRU_BLOCK ** -0.5),
        "b_gate_x": nrm(ks[8], (L, LRU_WIDTH), 0.01),
        "lru_lambda": lru_lambda,
        "lambda_q1": nrm(ks[11], (L, ATT_HEAD_DIM), 0.1),
        "lambda_k1": nrm(ks[12], (L, ATT_HEAD_DIM), 0.1),
        "lambda_q2": nrm(ks[13], (L, ATT_HEAD_DIM), 0.1),
        "lambda_k2": nrm(ks[14], (L, ATT_HEAD_DIM), 0.1),
        "att_head_norm": gain(ks[15], ATT_V_DIM),
        "w_out": nrm(ks[16], (L, D_MIX, D_MODEL), D_MIX ** -0.5),
        "norm_mix_post": gain(ks[17], D_MODEL),
        "norm_mlp_pre": gain(ks[18], D_MODEL),
        "w_up": nrm(ks[19], (L, D_MODEL, D_FF), D_MODEL ** -0.5),
        "w_down": nrm(ks[20], (L, D_FF, D_MODEL), D_FF ** -0.5),
        "norm_mlp_post": gain(ks[21], D_MODEL),
    }

def reference(x, norm_mix_pre, w_in, conv_w, conv_b, w_gate_a, b_gate_a, w_gate_x, b_gate_x,
              lru_lambda, lambda_q1, lambda_k1, lambda_q2, lambda_k2, att_head_norm, w_out,
              norm_mix_post, norm_mlp_pre, w_up, w_down, norm_mlp_post):
    splits = [LRU_WIDTH, 2 * LRU_WIDTH, 2 * LRU_WIDTH + ATT_WIDTH, 2 * LRU_WIDTH + 2 * ATT_WIDTH]
    for l in range(DEPTH):
        hn = rms_norm(x, norm_mix_pre[l])
        proj = jnp.einsum("btd,de->bte", hn, w_in[l])
        lru_x, lru_gate, q, k, v = jnp.split(proj, splits, axis=-1)
        y_lru = rglru_group(lru_x, lru_gate, conv_w[l], conv_b[l], w_gate_a[l], b_gate_a[l],
                            w_gate_x[l], b_gate_x[l], lru_lambda[l])
        y_att = diff_attn_group(q, k, v, lambda_q1[l], lambda_k1[l], lambda_q2[l], lambda_k2[l],
                                att_head_norm[l], lambda_init(l))
        mixed = jnp.concatenate([y_lru, y_att], axis=-1)
        x = x + rms_norm(jnp.einsum("bte,ed->btd", mixed, w_out[l]), norm_mix_post[l])
        hm = rms_norm(x, norm_mlp_pre[l])
        act = jnp.square(jax.nn.relu(jnp.einsum("btd,df->btf", hm, w_up[l])))
        x = x + rms_norm(jnp.einsum("btf,fd->btd", act, w_down[l]), norm_mlp_post[l])
    return x


_drawn_inputs = setup_inputs


def setup_inputs(seed=0):
    import zlib

    import numpy as np

    out = dict(_drawn_inputs(seed))
    spreads = {}
    factors = {'b_gate_a': 64.0,
     'b_gate_x': 64.0,
     'att_head_norm': 4.179,
     'norm_mix_post': 10.267,
     'norm_mlp_pre': 40.568,
     'norm_mlp_post': 54.55,
     'conv_b': 5.164}
    for name, (base, spread) in spreads.items():
        noise = np.random.default_rng([zlib.crc32(name.encode()), seed]).standard_normal(out[name].shape)
        drawn = base * np.exp(spread * noise) if base else spread * noise
        out[name] = __import__('jax').numpy.asarray(drawn.astype(out[name].dtype))
    for name, factor in factors.items():
        out[name] = (out[name] * factor).astype(out[name].dtype)
    return out
```

```python
import math
from contextlib import ExitStack

import numpy as np

import concourse.bass as bass
from concourse import mybir

F32 = mybir.dt.float32
F32R = mybir.dt.float32r
ACT = mybir.ActivationFunctionType
ALU = mybir.AluOpType
AX = mybir.AxisListType

P = 128
D = 1024
T = 1024
KC = D // P
TT = T // P
HALF = 512
LRU = D // 2
LC = LRU // P
HEADS = 4
FF = 4 * D
TAPS = 4
EPS = 1e-6
LAM_INIT = 0.8 - 0.6 * math.exp(-0.3 * 0)
Q_SCALE = 64 ** -0.5
LRU_C = 8.0
GELU_A = 0.044715
GELU_S = 2.0 * math.sqrt(2.0 / math.pi)
MASKED = -1e30

N_LRU = 2 * LC
N_V = 4
N_QK = 2 * HEADS
N_OUT = 8
P_V = N_LRU
P_QK = P_V + N_V
P_OUT = P_QK + N_QK
P_UP = P_OUT + N_OUT
GROUPS = FF // (2 * P)
PIECES = P_UP + 4 * GROUPS

C_GPRE, C_GMLP = 0, KC
C_CONVW = 2 * KC
C_CONVB = C_CONVW + TAPS * LC
C_BA = C_CONVB + LC
C_BX = C_BA + LC
C_LAM = C_BX + LC
C_HEADG = C_LAM + LC
NCOLS = C_HEADG + 1


def build(nc, x, weights, gate_weights, columns, lam_rows, post_gains, rope, constants, y_spill, out):
    with ExitStack() as ctx:
        ctx.enter_context(nc.allow_non_contiguous_dma(reason="small parameters"))
        base = (nc.sbuf_base + 63) // 64 * 64
        KB = 1024

        at_x = base
        at_y = at_x + 64 * KB
        at_v = at_y + 64 * KB
        at_w = at_v + 32 * KB
        at_s = at_w + 24 * KB
        at_c = at_s + 20 * KB

        def sb(name, shape, dt, offset):
            return nc.alloc_sbuf_tensor_at(name, shape, dt, offset=offset)

        xh = sb("xh", [P, KC, T], F32R, at_x)
        xl = sb("xl", [P, KC, T], F32R, at_x + 32 * KB)
        probs = sb("probs", [P, 2, 2, T], F32, at_x)
        yacc = [sb("yacc0", [P, 4, D], F32, at_x + 16 * KB), sb("yacc1", [P, 4, D], F32, at_x + 48 * KB)]
        hm_s = sb("hm_s", [P, TT, D], F32, at_x)
        yh = sb("yh", [P, KC, T], F32R, at_y)
        yl = sb("yl", [P, KC, T], F32R, at_y + 32 * KB)
        u_t = sb("u_t", [P, LC, T], F32, at_y)
        gel = sb("gel", [P, LC, T], F32, at_y + 16 * KB)
        xc_t = sb("xc_t", [P, LC, T], F32, at_y + 32 * KB)
        dec = sb("dec", [P, LC, T], F32, at_y + 48 * KB)
        o_raw = sb("o_raw", [P, KC, T], F32, at_y)
        lru_raw = sb("lru_raw", [P, LC, T], F32, at_y + 32 * KB)
        x_sb = sb("x_sb", [P, TT, D], F32, at_v)
        vh = sb("vh", [P, TT, HALF], F32R, at_v)
        vl = sb("vl", [P, TT, HALF], F32R, at_v + 16 * KB)
        h_sb = sb("h_sb", [P, TT, D], F32, at_v)
        raw = [sb(f"raw{s}", [P, D], F32, at_w + 4 * s * KB) for s in range(2)]
        wh = [sb(f"wh{s}", [P, D], F32R, at_w + (8 + 4 * s) * KB) for s in range(2)]
        wl = [sb(f"wl{s}", [P, D], F32R, at_w + (16 + 4 * s) * KB) for s in range(2)]
        xch = sb("xch", [P, T], F32R, at_s)
        xcl = sb("xcl", [P, T], F32R, at_s + 4 * KB)
        lru_a = sb("lru_a", [P, T], F32, at_s + 8 * KB)
        lru_g = sb("lru_g", [P, T], F32, at_s + 12 * KB)
        gwh = sb("gwh", [P, 2, P], F32R, at_s + 16 * KB)
        gwl = sb("gwl", [P, 2, P], F32R, at_s + 17 * KB)
        lru_y = sb("lru_y", [P, T], F32, at_s + 12 * KB)
        cos_t = sb("cos_t", [P, 2, T], F32, at_s)
        q_sb = sb("q_sb", [P, 2, T], F32, at_s + 8 * KB)
        q_rot = sb("q_rot", [P, T], F32, at_s + 16 * KB)
        wt2h = sb("wt2h", [P, TT, 2 * P], F32R, at_s)
        wt2l = sb("wt2l", [P, TT, 2 * P], F32R, at_s + 8 * KB)
        o_sq = sb("o_sq", [P, 2, 2 * P], F32, at_s + 16 * KB)
        diag = sb("diag", [P, 2, T], F32, at_s)
        g_post = sb("g_post", [P, D], F32, at_s)
        x_re = sb("x_re", [P, 2, D], F32, at_s + 4 * KB)
        junk = sb("junk", [P, D], F32, at_s + 12 * KB)
        junk2 = sb("junk2", [P, D], F32, at_s + 16 * KB)
        wdh = sb("wdh", [P, 2, D], F32R, at_s)
        wdl = sb("wdl", [P, 2, D], F32R, at_s + 8 * KB)
        relu = sb("relu", [P, 2, HALF], F32, at_s + 16 * KB)
        g_out = sb("g_out", [P, D], F32, at_w)
        out_junk = sb("out_junk", [P, D], F32, at_w + 4 * KB)

        small_at = [at_c]

        def small(name, shape, dt=F32):
            t = sb(name, shape, dt, small_at[0])
            n = 4
            for s in shape[1:]:
                n *= s
            small_at[0] += (n + 31) // 32 * 32
            assert small_at[0] <= nc.sbuf_usable_end
            return t

        ident = small("ident", [P, P])
        ident_r = small("ident_r", [P, P], F32R)
        mask_r = small("mask_r", [P, P], F32R)
        ones = small("ones", [P, P])
        cols = small("cols", [P, NCOLS])
        spl = small("spl", [P, 2, LC])
        tiny = small("tiny", [P, 6, LC])
        lam_e = small("lam_e", [P, 4])
        mean_sq = small("mean_sq", [P, 4, TT])
        var = small("var", [P, TT])
        root = small("root", [P, TT])
        t1 = small("t1", [P, TT])
        t2 = small("t2", [P, TT])
        rstd = small("rstd", [P, 4, TT])
        head_gain = small("head_gain", [P, 1])
        negmax = small("negmax", [P, 2, 2])
        denom = small("denom", [P, 2, 2])
        recip = small("recip", [P, 2])
        hvar = small("hvar", [P, 32])
        hroot = small("hroot", [P, 32])
        ht1 = small("ht1", [P, 32])
        ht2 = small("ht2", [P, 32])
        hrstd = small("hrstd", [P, 32])
        gw_raw = sb("gw_raw", [P, LC, 2, P], F32, at_v)
        lam_raw = sb("lam_raw", [P, 4, 64], F32, at_s + 18 * KB)
        mask_raw = sb("mask_raw", [P, P], F32, at_s + 19 * KB)

        pair = [ctx.enter_context(nc.psum_tensor(f"pair{j}", [P, 2 * HALF], F32)) for j in range(4)]

        def bank(b):
            return pair[b // 2][:, HALF * (b % 2):HALF * (b % 2) + HALF]

        def sem(name):
            return ctx.enter_context(nc.semaphore(name))

        x_loaded = [sem(f"x_loaded{i}") for i in range(4)]
        small_loaded = sem("small_loaded")
        gates_loaded = sem("gates_loaded")
        raw_loaded = [sem(f"raw_loaded{s}") for s in range(2)]
        w_hi = sem("w_hi")
        w_lo = sem("w_lo")
        piece_used = sem("piece_used")
        const_ready = sem("const_ready")
        lam_step = sem("lam_step")
        act_step = sem("act_step")
        dve_step = sem("dve_step")
        dve_chain = sem("dve_chain")
        conv_step = sem("conv_step")
        gelu_step = sem("gelu_step")
        scan_step = sem("scan_step")
        rope_step = sem("rope_step")
        squares = sem("squares")
        var_ready = sem("var_ready")
        root_ready = sem("root_ready")
        scaled = sem("scaled")
        tr_done = sem("tr_done")
        tr_hi = sem("tr_hi")
        tr_lo = sem("tr_lo")
        lru_copied = sem("lru_copied")
        conv_done = sem("conv_done")
        xc_hi = sem("xc_hi")
        xc_lo = sem("xc_lo")
        gates_done = sem("gates_done")
        sig_done = sem("sig_done")
        gelu_in = sem("gelu_in")
        gelu_sq = sem("gelu_sq")
        gelu_sig = sem("gelu_sig")
        gelu_done = sem("gelu_done")
        tanh_done = sem("tanh_done")
        ix_done = sem("ix_done")
        decay_done = sem("decay_done")
        decay_sq = sem("decay_sq")
        bsq_done = sem("bsq_done")
        sqrt_done = sem("sqrt_done")
        lru_done = sem("lru_done")
        lru_spilled = sem("lru_spilled")
        lru_back = sem("lru_back")
        v_hi = sem("v_hi")
        v_lo = sem("v_lo")
        rope_loaded = sem("rope_loaded")
        q_copied = sem("q_copied")
        rot_loaded = sem("rot_loaded")
        rope_sum = sem("rope_sum")
        qk_hi = sem("qk_hi")
        qk_lo = sem("qk_lo")
        scores = sem("scores")
        maxed = sem("maxed")
        exped = sem("exped")
        w_done = sem("w_done")
        wt_done = sem("wt_done")
        wt_hi = sem("wt_hi")
        wt_lo = sem("wt_lo")
        pv_done = sem("pv_done")
        o_copied = sem("o_copied")
        o_squared = sem("o_squared")
        sumsq_done = sem("sumsq_done")
        head_var = sem("head_var")
        head_root = sem("head_root")
        diag_done = sem("diag_done")
        spread_done = sem("spread_done")
        o_norm = sem("o_norm")
        mix_hi = sem("mix_hi")
        mix_lo = sem("mix_lo")
        out_bank = sem("out_bank")
        y_copied = sem("y_copied")
        y_squared = sem("y_squared")
        post_var = sem("post_var")
        post_root = sem("post_root")
        x_back = [sem(f"x_back{i}") for i in range(2)]
        g_post_loaded = sem("g_post_loaded")
        h_done = sem("h_done")
        h_squared = sem("h_squared")
        pre_var = sem("pre_var")
        pre_root = sem("pre_root")
        pre_rstd = sem("pre_rstd")
        hm_scaled = sem("hm_scaled")
        acc_zero = sem("acc_zero")
        up_done = sem("up_done")
        relu_done = sem("relu_done")
        act_hi = sem("act_hi")
        relu_sq = sem("relu_sq")
        act_lo = sem("act_lo")
        down_done = sem("down_done")
        y_added = sem("y_added")
        fin_sq = sem("fin_sq")
        fin_var = sem("fin_var")
        fin_root = sem("fin_root")
        g_out_loaded = sem("g_out_loaded")
        fin_done = sem("fin_done")
        stored = sem("stored")

        block = ctx.enter_context(nc.Block())

        def mm3(pe, o, a_hi, a_lo, b_hi, b_lo, first, last):
            pe.matmul(o, a_hi, b_hi, start=first, stop=False)
            pe.matmul(o, a_hi, b_lo, start=False, stop=False)
            return pe.matmul(o, a_lo, b_hi, start=False, stop=last)

        def pieces_of(t):
            return t[:, :].rearrange("p (k c) -> p k c", c=P)

        @block.sync
        def _(sp):
            for i in range(4):
                sp.dma_start(x_sb[:, 2 * i:2 * i + 2, :],
                             x[0].rearrange("(t p) d -> p t d", p=P)[:, 2 * i:2 * i + 2, :]).then_inc(x_loaded[i], 16)
            for s in range(2):
                sp.dma_start(raw[s][:, :], weights[s]).then_inc(raw_loaded[s], 16)
            with sp.Fori(0, PIECES // 2 - 1) as i:
                for s in range(2):
                    sp.wait_ge(w_lo, 2 * i + s + 1)
                    sp.dma_start(raw[s][:, :], weights[2 * i + s + 2]).then_inc(raw_loaded[s], 16)
            sp.wait_ge(w_lo, PIECES)
            sp.dma_start(g_out[:, :], post_gains[1].partition_broadcast(P)).then_inc(g_out_loaded, 16)
            for t in range(TT):
                sp.wait_ge(fin_done, t + 1)
                sp.dma_start(out[0, P * t:P * t + P, :], h_sb[:, t, :]).then_inc(stored, 16)
            sp.wait_ge(stored, 16 * TT)

        @block.gpsimd
        def _(pool):
            pool.dma_start(cols[:, :], columns).then_inc(small_loaded, 16)
            pool.dma_start(ident[:, :], constants[0]).then_inc(small_loaded, 16)
            pool.dma_start(mask_raw[:, :], constants[1]).then_inc(small_loaded, 16)
            pool.dma_start(lam_raw[:, :, :], lam_rows.partition_broadcast(P)).then_inc(small_loaded, 16)
            pool.wait_ge(tr_done, 16)
            pool.dma_start(gw_raw[:, :, :, :], gate_weights).then_inc(gates_loaded, 16)
            for c in range(LC):
                pool.wait_ge(lru_done, c + 1)
                pool.dma_start(y_spill[c], lru_y[:, :]).then_inc(lru_spilled, 16)
            pool.wait_ge(lru_spilled, 16 * LC)
            pool.dma_start(cos_t[:, :, :], rope).then_inc(rope_loaded, 16)
            pool.wait_ge(scores, 2 * 8 * HEADS)
            pool.dma_start(lru_raw[:, :, :], y_spill.rearrange("c p t -> p c t")).then_inc(lru_back, 16)
            pool.wait_ge(spread_done, 2 * HEADS)
            pool.dma_start(g_post[:, :], post_gains[0].partition_broadcast(P)).then_inc(g_post_loaded, 16)
            for t in range(TT):
                if t >= 2:
                    pool.wait_ge(h_done, t - 1)
                pool.dma_start(x_re[:, t % 2, :], x[0, P * t:P * t + P, :]).then_inc(x_back[t % 2], 16)
            pool.wait_ge(tr_done, 32)
            nc.gpsimd.memset(yacc[0][:, :, :], 0.0).then_inc(acc_zero, 1)
            nc.gpsimd.memset(yacc[1][:, :, :], 0.0).then_inc(acc_zero, 1)

        @block.tensor
        def _(pe):
            def transposes(src, round_):
                for hf in range(2):
                    pe.wait_ge(scaled if round_ == 0 else hm_scaled, 4 * (hf + 1))
                    for k in range(KC):
                        n = 16 * round_ + 8 * hf + k
                        if n % 16 >= 8:
                            pe.wait_ge(tr_lo, n - 7)
                        for t in range(4):
                            mm = pe.transpose(bank(k)[:, P * t:P * t + P],
                                              src[:, 4 * hf + t, P * k:P * k + P], ident[:, :])
                        mm.then_inc(tr_done, 1)

            def feature_piece(slot, out_pair, rh, rl):
                for hf in range(2):
                    o = out_pair[:, HALF * hf:HALF * hf + HALF]
                    for k in range(KC):
                        cols_ = slice(HALF * hf, HALF * hf + HALF)
                        mm = mm3(pe, o, pieces_of(wh[slot])[:, k, :], pieces_of(wl[slot])[:, k, :],
                                 rh[:, k, cols_], rl[:, k, cols_], k == 0, k == KC - 1)
                    yield mm

            def token_piece(slot, j, banks_copied):
                for kk in range(2):
                    k = 2 * j + kk
                    w_cols = slice(HALF * kk, HALF * kk + HALF)
                    for t in range(TT):
                        tok = slice(P * t, P * t + P)
                        if k == 0 and banks_copied:
                            pe.wait_ge(y_copied, t + 1)
                        mm = mm3(pe, bank(t), xh[:, k, tok], xl[:, k, tok], wh[slot][:, w_cols],
                                 wl[slot][:, w_cols], k == 0, k == KC - 1)
                        if k == KC - 1:
                            mm.then_inc(out_bank, 1)
                if j < KC // 2 - 1:
                    mm.then_inc(piece_used, 1)

            pe.wait_ge(small_loaded, 64)
            transposes(x_sb, 0)
            with pe.Fori(0, LC) as c:
                for s in range(2):
                    pe.wait_ge(w_lo, 2 * c + s + 1)
                    if s == 0:
                        pe.wait_ge(tr_lo, 16)
                    for mm in feature_piece(s, pair[s], xh, xl):
                        pass
                    mm.then_inc(piece_used, 1)
                pe.wait_ge(xc_lo, c + 1)
                for g in range(2):
                    for hf in range(2):
                        tok = slice(HALF * hf, HALF * hf + HALF)
                        mm = mm3(pe, pair[2 + g][:, tok], gwh[:, g, :], gwl[:, g, :], xch[:, tok],
                                 xcl[:, tok], True, True)
                    mm.then_inc(gates_done, 1)
            pe.wait_ge(lru_copied, 2 * LC)
            pe.wait_ge(sig_done, 2 * LC)
            for j in range(N_V):
                pe.wait_ge(w_lo, P_V + j + 1)
                token_piece(j % 2, j, False)
            with pe.Fori(0, HEADS) as h:
                for s in range(2):
                    pe.wait_ge(w_lo, 2 * h + P_QK + s + 1)
                    if s == 0:
                        pe.wait_ge(v_lo, TT // 2)
                    for mm in feature_piece(s, pair[s], xh, xl):
                        pass
                    mm.then_inc(piece_used, 1)
            pe.wait_ge(const_ready, 1)
            pe.wait_ge(act_step, 1)
            pe.wait_ge(v_lo, TT)
            groups_before = [0]

            def score_step(s):
                h, i = divmod(s, TT)
                if i == 0:
                    pe.wait_ge(qk_lo, 2 * (h + 1))
                q_tok = slice(P * i, P * i + P)
                for m in range(2):
                    rows = slice(64 * m, 64 * m + 64)
                    if s == 0:
                        pe.wait_ge(q_copied, 2 * HEADS)
                    else:
                        pe.wait_ge(exped, 2 * (s - 1) + m + 1)
                    n_banks = i // 4 + 1
                    for b in range(n_banks):
                        k_hi = min(P * (i + 1), HALF * (b + 1))
                        keys = slice(HALF * b, k_hi)
                        last = b == n_banks - 1
                        mm = mm3(pe, pair[m][:, keys], yh[rows, 2 * h, q_tok], yl[rows, 2 * h, q_tok],
                                 yh[rows, 2 * h + 1, keys], yl[rows, 2 * h + 1, keys], True, not last)
                        if last:
                            mm = pe.matmul(pair[m][:, P * i:P * i + P], ident_r[:, :], mask_r[:, :],
                                           start=False, stop=True)
                    mm.then_inc(scores, 1)

            def transpose_step(s):
                i = s % TT
                pe.wait_ge(w_done, s + 1)
                for b in range(i // 4 + 1):
                    g = groups_before[0]
                    if g >= 2:
                        pe.wait_ge(wt_lo, g - 1)
                    for kb in range(4 * b, min(4 * b + 4, i + 1)):
                        mm = pe.transpose(bank(4 + g % 2)[:, P * (kb - 4 * b):P * (kb - 4 * b) + P],
                                          probs[:, s % 2, 0, P * kb:P * kb + P], ident[:, :])
                    mm.then_inc(wt_done, 1)
                    groups_before[0] += 1

            def pv_step(j):
                h, jj = divmod(j, TT // 2)
                pe.wait_ge(wt_lo, groups_before[0])
                if j >= 1:
                    pe.wait_ge(o_copied, j)
                th, tl = (xl[:, 0:2, :], xl[:, 2:4, :]) if j % 2 == 0 else (wt2h, wt2l)
                if j % 2 == 0:
                    th = th.rearrange("p a (b q) -> p (a b) q", q=2 * P)
                    tl = tl.rearrange("p a (b q) -> p (a b) q", q=2 * P)
                n = 2 * jj + 2
                e = slice(P * h, P * h + P)
                for kb in range(n):
                    q0 = P if kb == n - 1 else 0
                    mm = mm3(pe, bank(6)[:, q0:2 * P], vh[:, kb, e], vl[:, kb, e], th[:, kb, q0:],
                             tl[:, kb, q0:], kb == 0, kb == n - 1)
                mm.then_inc(pv_done, 1)

            def sumsq_step(j):
                pe.wait_ge(o_squared, j + 1)
                for i in range(2):
                    col = 2 * j + i
                    mm = pe.matmul(bank(7)[:, col:col + 1], o_sq[:, j % 2, P * i:P * i + P], ones[:, 0:1],
                                   start=True, stop=True)
                mm.then_inc(sumsq_done, 1)

            steps = TT * HEADS
            for s in range(steps + 1):
                if s < steps:
                    score_step(s)
                if s >= 1:
                    transpose_step(s - 1)
                    if s % 2 == 0:
                        pv_step(s // 2 - 1)
                    if s % 2 == 1 and s >= 3:
                        sumsq_step((s - 1) // 2 - 1)
            sumsq_step(steps // 2 - 1)
            for h in range(HEADS):
                pe.wait_ge(diag_done, h + 1)
                if h >= 2:
                    pe.wait_ge(o_norm, h - 1)
                for hf in range(2):
                    mm = pe.matmul(pair[h % 2][:, HALF * hf:HALF * hf + HALF], ones[:, :],
                                   diag[:, h % 2, HALF * hf:HALF * hf + HALF], start=True, stop=True)
                    mm.then_inc(spread_done, 1)
            pe.wait_ge(mix_lo, 2 * LC)
            for j in range(N_OUT):
                pe.wait_ge(w_lo, P_OUT + j + 1)
                token_piece(j % 2, j % 4, j >= 4)
            pe.wait_ge(y_copied, 2 * TT)
            transposes(hm_s, 1)

            def up(g2):
                for cc in range(2):
                    f = g2 + cc
                    if isinstance(g2, int) and g2 == 0:
                        pe.wait_ge(w_lo, P_UP + cc + 1)
                    else:
                        pe.wait_ge(w_lo, 2 * g2 + (P_UP - 2) + cc + 1)
                    n = 0
                    for mm in feature_piece(cc, pair[cc], yh, yl):
                        mm.then_inc(up_done, 1)
                        n += 1

            def up_waits(g2):
                pe.wait_ge(relu_done, 2 * g2)

            def down(g, par, wait_piece):
                pe.wait_ge(act_lo, 4 * g + 4)
                pe.wait_ge(w_lo, wait_piece)
                for t in range(TT):
                    if t >= 2:
                        pe.wait_ge(y_added, 8 * g + t - 1)
                    elif not (isinstance(g, int) and g == 0):
                        pe.wait_ge(y_added, 8 * g + t - 1)
                    tok = slice(P * t, P * t + P)
                    for hf in range(2):
                        o = pair[2 + t % 2][:, HALF * hf:HALF * hf + HALF]
                        for cc in range(2):
                            a = 2 * par + cc
                            mm = mm3(pe, o, xh[:, a, tok], xl[:, a, tok],
                                     wdh[:, cc, HALF * hf:HALF * hf + HALF],
                                     wdl[:, cc, HALF * hf:HALF * hf + HALF], cc == 0, cc == 1)
                    mm.then_inc(down_done, 1)

            pe.wait_ge(tr_lo, 32)
            up(0)
            up_waits(2)
            up(2)
            down(0, 0, P_UP + 6)
            with pe.Fori(0, (GROUPS - 2) // 2) as i:
                for par in range(2):
                    g = 2 * i + par + 1
                    up_waits(2 * g + 2)
                    up(2 * g + 2)
                    down(g, 1 - par, 4 * g + P_UP + 6)
            down(GROUPS - 1, (GROUPS - 1) % 2, PIECES)

        @block.scalar
        def _(act):
            def hi(p, dst, slot_wait=None):
                s = slot_wait[2]
                act.wait_ge(raw_loaded[s], slot_wait[3])
                if slot_wait[0] is not None:
                    act.wait_ge(slot_wait[0], slot_wait[1])
                act.activation(dst, raw[s][:, :], ACT.Copy).then_inc(w_hi, 1)

            def hi_early(p):
                free = None if p < 2 else p - 1
                hi(p, wh[p % 2][:, :], (piece_used if free else None, free, p % 2, 16 * (p // 2 + 1)))

            act.wait_ge(small_loaded, 64)
            act.activation(ident_r[:, :], ident[:, :], ACT.Copy)
            act.activation(mask_r[:, :], mask_raw[:, :], ACT.Copy).then_inc(act_step, 1)
            hi_early(0)
            hi_early(1)
            for t in range(TT):
                if t % 2 == 0:
                    act.wait_ge(x_loaded[t // 2], 16)
                if t >= 2:
                    act.wait_ge(squares, t - 1)
                act.activation(u_t[:, t % 2, :], x_sb[:, t, :], ACT.Square,
                               accum_out=mean_sq[:, 0, t:t + 1]).then_inc(squares, 1)
                if t % 4 == 3:
                    act.wait_ge(var_ready, t // 4 + 1)
                    act.activation(root[:, t - 3:t + 1], var[:, t - 3:t + 1], ACT.Sqrt).then_inc(root_ready, 1)

            def split_hi(n0, dst, gain0):
                for hf in range(2):
                    for k in range(KC):
                        n = n0 + 8 * hf + k
                        act.wait_ge(tr_done, n + 1)
                        act.activation(dst[:, k, HALF * hf:HALF * hf + HALF], bank(k), ACT.Copy,
                                       scale=cols[:, gain0 + k:gain0 + k + 1]).then_inc(tr_hi, 1)

            split_hi(0, xh, C_GPRE)
            act.wait_ge(lam_step, 1)
            act.activation(lam_e[:, 2:4], lam_e[:, 0:2], ACT.Exp)
            act.activation(tiny[:, 1, :], tiny[:, 0, :], ACT.Exp, scale=-1.0).then_inc(act_step, 1)
            act.wait_ge(gates_loaded, 16)
            act.wait_ge(dve_step, 1)
            for c in range(LC):
                act.wait_ge(piece_used, 2 * c + 1)
                act.activation(u_t[:, c, :], pair[0][:, :], ACT.Copy).then_inc(lru_copied, 1)
                hi(None, wh[0][:, :], (piece_used, 2 * c + 1, 0, 16 * c + 32))
                act.wait_ge(conv_done, c + 1)
                act.activation(gwh[:, :, :], gw_raw[:, c, :, :], ACT.Copy)
                act.activation(xch[:, :], xc_t[:, c, :], ACT.Copy).then_inc(xc_hi, 1)
                act.wait_ge(piece_used, 2 * c + 2)
                act.activation(gel[:, c, :], pair[1][:, :], ACT.Copy).then_inc(lru_copied, 1)
                act.wait_ge(lru_copied, 2 * c + 2)
                act.wait_ge(gelu_done, c)
                act.activation(lru_g[:, :], gel[:, c, :], ACT.Square).then_inc(gelu_sq, 1)
                hi(None, wh[1][:, :], (piece_used, 2 * c + 2, 1, 16 * c + 32))
                act.wait_ge(gates_done, 2 * c + 1)
                act.activation(dec[:, c, :], pair[2][:, :], ACT.Sigmoid,
                               bias=cols[:, bass.ds(c + C_BA, 1)]).then_inc(sig_done, 1)
                act.wait_ge(gates_done, 2 * c + 2)
                act.wait_ge(ix_done, c)
                act.activation(lru_a[:, :], pair[3][:, :], ACT.Sigmoid,
                               bias=cols[:, bass.ds(c + C_BX, 1)]).then_inc(sig_done, 1)
                act.wait_ge(gelu_in, c + 1)
                act.activation(lru_g[:, :], lru_g[:, :], ACT.Sigmoid, scale=GELU_S).then_inc(gelu_sig, 1)
                act.wait_ge(sig_done, 2 * c + 2)
                act.activation(u_t[:, c, :], dec[:, c, :], ACT.Tanh,
                               scale=spl[:, 0, bass.ds(c, 1)]).then_inc(tanh_done, 1)
            act.wait_ge(tanh_done, LC)
            for c in range(LC):
                act.activation(dec[:, c, :], dec[:, c, :], ACT.Exp,
                               scale=spl[:, 1, bass.ds(c, 1)]).then_inc(decay_done, 1)
                act.wait_ge(decay_done, c + 1)
                act.wait_ge(bsq_done, c)
                act.wait_ge(ix_done, LC)
                act.activation(lru_a[:, :], dec[:, c, :], ACT.Square).then_inc(decay_sq, 1)
            act.wait_ge(bsq_done, LC)
            hi_early(P_V + 2)
            for c in range(LC):
                act.activation(u_t[:, c, :], u_t[:, c, :], ACT.Sqrt).then_inc(sqrt_done, 1)
            hi_early(P_V + 3)
            for t in range(TT):
                act.wait_ge(out_bank, t + 1)
                act.activation(vh[:, t, :], bank(t), ACT.Copy).then_inc(v_hi, 1)
            for n in range(2):
                act.wait_ge(out_bank, TT)
                hi(None, wh[n][:, :], (piece_used, P_V + N_V - 1, n, 16 * ((P_QK + n) // 2 + 1)))
            for h in range(HEADS):
                for s in range(2):
                    act.wait_ge(piece_used, 2 * h + P_QK + s)
                    act.wait_ge(rope_loaded, 16)
                    act.wait_ge(qk_lo, 2 * h)
                    act.activation(q_sb[:, s, :], pair[s][:, :], ACT.Copy).then_inc(q_copied, 1)
                    act.wait_ge(q_copied, 2 * h + s + 1)
                    if s == 1:
                        act.wait_ge(rope_sum, 2 * h + 1)
                    for m in range(2):
                        a, b = 64 * m, 64 * m + 32
                        act.dma_start(q_rot[a:a + 32, :], q_sb[b:b + 32, s, :]).then_inc(rot_loaded, 16)
                        act.dma_start(q_rot[b:b + 32, :], q_sb[a:a + 32, s, :]).then_inc(rot_loaded, 16)
                    hi(None, wh[s][:, :], (piece_used, 2 * h + P_QK + s, s, 16 * h + 16 * (P_QK // 2 + 2)))
                    act.wait_ge(rope_sum, 2 * h + s + 1)
                    act.activation(yh[:, 2 * h + s, :], q_sb[:, s, :], ACT.Copy,
                                   scale=Q_SCALE if s == 0 else 1.0).then_inc(qk_hi, 1)
            steps = TT * HEADS
            seen = [0]
            for s in range(steps + 1):
                if s >= 1:
                    p, i = s - 1, (s - 1) % TT
                    j = p // 2
                    th = xl[:, 0:2, :].rearrange("p a (b q) -> p (a b) q", q=2 * P) if j % 2 == 0 else wt2h
                    for b in range(i // 4 + 1):
                        act.wait_ge(wt_done, seen[0] + 1)
                        if j >= 2:
                            act.wait_ge(pv_done, j - 1)
                        nb = min(4, i + 1 - 4 * b)
                        act.activation(th[:, 4 * b:4 * b + nb, P * (p % 2):P * (p % 2) + P],
                                       bank(4 + seen[0] % 2)[:, 0:P * nb].rearrange("p (k q) -> p k q", q=P),
                                       ACT.Copy).then_inc(wt_hi, 1)
                        seen[0] += 1
                if s < steps:
                    i = s % TT
                    for m in range(2):
                        act.wait_ge(maxed, 2 * s + m + 1)
                        if s >= 2:
                            act.wait_ge(wt_done, seen[0])
                        act.activation(probs[:, s % 2, m, 0:P * (i + 1)], pair[m][:, 0:P * (i + 1)], ACT.Exp,
                                       bias=negmax[:, s % 2, m:m + 1],
                                       accum_out=denom[:, s % 2, m:m + 1]).then_inc(exped, 1)
                if s % 2 == 0 and s >= 2:
                    j = s // 2 - 1
                    h, jj = divmod(j, TT // 2)
                    q = slice(2 * P * jj, 2 * P * jj + 2 * P)
                    act.wait_ge(pv_done, j + 1)
                    act.activation(o_raw[:, 2 * h, q], bank(6)[:, 0:2 * P], ACT.Copy).then_inc(o_copied, 1)
                    act.wait_ge(o_copied, j + 1)
                    if j >= 2:
                        act.wait_ge(sumsq_done, j - 1)
                    act.activation(o_sq[:, j % 2, :], o_raw[:, 2 * h, q], ACT.Square).then_inc(o_squared, 1)
            act.wait_ge(head_var, 1)
            act.activation(hroot[:, :], hvar[:, :], ACT.Sqrt).then_inc(head_root, 1)
            for h in range(HEADS):
                act.wait_ge(o_norm, h + 1)
                act.activation(xh[:, LC + h, :], o_raw[:, 2 * h, :], ACT.Copy).then_inc(mix_hi, 1)
            act.wait_ge(lru_back, 16)
            for c in range(LC):
                act.activation(xh[:, c, :], lru_raw[:, c, :], ACT.Copy).then_inc(mix_hi, 1)
            for half in range(2):
                for j in range(2, 4):
                    p = P_OUT + 4 * half + j
                    hi(p, wh[p % 2][:, :], (piece_used, p - 2 - half, p % 2, 16 * (p // 2 + 1)))
                for t in range(TT):
                    n = TT * (1 + half) + t
                    act.wait_ge(out_bank, n + 1)
                    act.activation(h_sb[:, t, HALF * half:HALF * half + HALF], bank(t),
                                   ACT.Copy).then_inc(y_copied, 1)
                for j in range(2):
                    p = P_OUT + 4 * half + 4 + j
                    hi(p, wh[p % 2][:, :], (out_bank, TT * (2 + half), p % 2, 16 * (p // 2 + 1)))
            for gq in range(2):
                act.wait_ge(post_var, gq + 1)
                act.activation(root[:, 4 * gq:4 * gq + 4], var[:, 4 * gq:4 * gq + 4], ACT.Sqrt).then_inc(post_root, 1)
                for t in range(4 * gq, 4 * gq + 4):
                    act.wait_ge(h_done, t + 1)
                    act.wait_ge(h_squared, t)
                    act.activation(junk[:, :], h_sb[:, t, :], ACT.Square,
                                   accum_out=mean_sq[:, 2, t:t + 1]).then_inc(h_squared, 1)
                act.wait_ge(pre_var, gq + 1)
                act.activation(root[:, 4 * gq:4 * gq + 4], var[:, 4 * gq:4 * gq + 4], ACT.Sqrt).then_inc(pre_root, 1)
                act.wait_ge(pre_rstd, gq + 1)
                act.wait_ge(out_bank, 3 * TT)
                for t in range(4 * gq, 4 * gq + 4):
                    act.activation(hm_s[:, t, :], h_sb[:, t, :], ACT.Copy,
                                   scale=rstd[:, 2, t:t + 1]).then_inc(hm_scaled, 1)
            split_hi(16, yh, C_GMLP)

            def act_unit(g, par, cc, hf):
                n = 4 * g + 2 * cc + hf
                act.wait_ge(up_done, n + 1)
                if not (isinstance(g, int) and g == 0 and cc == 0):
                    act.wait_ge(act_lo, n - 1)
                act.activation(relu[:, hf, :], bank(2 * cc + hf), ACT.Relu).then_inc(relu_done, 1)
                act.wait_ge(relu_done, n + 1)
                act.activation(xh[:, 2 * par + cc, HALF * hf:HALF * hf + HALF], relu[:, hf, :],
                               ACT.Square).then_inc(act_hi, 1)

            def act_group(g, par, up_next, down_next):
                for cc in range(2):
                    act_unit(g, par, cc, 0)
                    act_unit(g, par, cc, 1)
                    if up_next:
                        hi(None, wh[cc][:, :], (up_done, 4 * g + 2 * cc + 2, cc, 32 * g + 16 * (P_UP // 2 + 2)))
                for cc in range(2):
                    late = 2 if up_next else 0
                    w = (None, None) if isinstance(g, int) and g == 0 else (down_done, 8 * g)
                    hi(None, wdh[:, cc, :], (*w, cc, 32 * g + 16 * (P_UP // 2 + 2 + late // 2)))

            act.wait_ge(h_done, TT)
            act.wait_ge(h_squared, TT)
            act_group(0, 0, True, True)
            with act.Fori(0, (GROUPS - 2) // 2) as i:
                for par in range(2):
                    act_group(2 * i + par + 1, 1 - par, True, True)
            act_group(GROUPS - 1, (GROUPS - 1) % 2, False, True)
            act.wait_ge(w_lo, PIECES)
            for t in range(TT):
                act.wait_ge(y_added, 8 * (GROUPS - 1) + t + 1)
                act.wait_ge(fin_sq, t)
                act.activation(out_junk[:, :], yacc[t // 4][:, t % 4, :], ACT.Square,
                               accum_out=mean_sq[:, 3, t:t + 1]).then_inc(fin_sq, 1)
                act.wait_ge(fin_var, t + 1)
                act.activation(root[:, t:t + 1], var[:, t:t + 1], ACT.Sqrt).then_inc(fin_root, 1)

        @block.vector
        def _(dve):
            chain = [0]

            def link(ins):
                chain[0] += 1
                ins.then_inc(dve_chain, 1)
                dve.wait_ge(dve_chain, chain[0])

            def lo(dst, src_hi, s, n):
                dve.wait_ge(w_hi, n)
                dve.tensor_tensor(dst, raw[s][:, :], src_hi.bitcast(F32), ALU.subtract).then_inc(w_lo, 1)

            def lo_early(p):
                lo(wl[p % 2][:, :], wh[p % 2][:, :], p % 2, p + 1)

            def rsqrt_pre(sums, v, n, signal):
                dve.tensor_scalar(v, sums, 1.0 / n, EPS, ALU.mult, ALU.add).then_inc(signal, 1)

            def rsqrt_post(v, r, a, b, result, signal=None):
                link(dve.reciprocal(a, r))
                link(dve.tensor_tensor(b, v, a, ALU.mult))
                link(dve.scalar_tensor_tensor(b, b, -0.5, a, ALU.mult, ALU.mult))
                ins = dve.scalar_tensor_tensor(result, b, 1.5, a, ALU.add, ALU.mult)
                ins.then_inc(signal, 1) if signal else link(ins)

            dve.memset(ones[:, :], 1.0).then_inc(const_ready, 1)
            dve.wait_ge(small_loaded, 64)
            link(dve.tensor_scalar(head_gain[:, :], cols[:, C_HEADG:C_HEADG + 1], 1.0 - LAM_INIT, None, ALU.mult))
            link(dve.tensor_scalar(tiny[:, 2, :], cols[:, C_LAM:C_LAM + LC], -1.0, None, ALU.mult))
            link(dve.tensor_tensor(tiny[:, 0, :], tiny[:, 2, :], cols[:, C_LAM:C_LAM + LC], ALU.max))
            for m in range(2):
                link(dve.tensor_tensor(lam_raw[:, 2 * m, :], lam_raw[:, 2 * m, :], lam_raw[:, 2 * m + 1, :], ALU.mult))
                link(dve.tensor_reduce(lam_e[:, m:m + 1], lam_raw[:, 2 * m, :], AX.X, ALU.add))
            dve.tensor_scalar(tiny[:, 2, :], tiny[:, 2, :], 0.0, None, ALU.max).then_inc(lam_step, 1)
            lo_early(0)
            lo_early(1)
            for gq in range(2):
                sl = slice(4 * gq, 4 * gq + 4)
                dve.wait_ge(squares, 4 * gq + 4)
                rsqrt_pre(mean_sq[:, 0, sl], var[:, sl], D, var_ready)
                dve.wait_ge(root_ready, gq + 1)
                rsqrt_post(var[:, sl], root[:, sl], t1[:, sl], t2[:, sl], rstd[:, 0, sl])
                for t in range(4 * gq, 4 * gq + 4):
                    dve.tensor_scalar(x_sb[:, t, :], x_sb[:, t, :], rstd[:, 0, t:t + 1], None,
                                      ALU.mult).then_inc(scaled, 1)

            def split_lo(n0, dst_h, dst_l, gain0):
                for hf in range(2):
                    for k in range(KC):
                        cols_ = slice(HALF * hf, HALF * hf + HALF)
                        dve.wait_ge(tr_hi, n0 + 8 * hf + k + 1)
                        dve.scalar_tensor_tensor(dst_l[:, k, cols_], bank(k), cols[:, gain0 + k:gain0 + k + 1],
                                                 dst_h[:, k, cols_].bitcast(F32), ALU.mult,
                                                 ALU.subtract).then_inc(tr_lo, 1)

            split_lo(0, xh, xl, C_GPRE)
            dve.wait_ge(act_step, 2)
            dve.wait_ge(lam_step, 1)
            link(dve.tensor_tensor(lam_e[:, 0:1], lam_e[:, 2:3], lam_e[:, 3:4], ALU.subtract))
            link(dve.tensor_scalar(lam_e[:, 1:2], lam_e[:, 0:1], -1.0, -LAM_INIT, ALU.mult, ALU.add))
            e_, z_, z2, acc = tiny[:, 1, :], tiny[:, 3, :], tiny[:, 4, :], tiny[:, 5, :]
            link(dve.tensor_scalar(z_, e_, 2.0, None, ALU.add))
            link(dve.reciprocal(acc, z_))
            link(dve.tensor_tensor(z_, e_, acc, ALU.mult))
            link(dve.tensor_tensor(z2, z_, z_, ALU.mult))
            link(dve.tensor_scalar(acc, z2, 1.0 / 17, 1.0 / 15, ALU.mult, ALU.add))
            for n in (13, 11, 9, 7, 5, 3, 1):
                link(dve.tensor_tensor(acc, acc, z2, ALU.mult))
                link(dve.tensor_scalar(acc, acc, 1.0 / n, None, ALU.add))
            link(dve.tensor_tensor(acc, acc, z_, ALU.mult))
            link(dve.scalar_tensor_tensor(acc, acc, 2.0, tiny[:, 2, :], ALU.mult, ALU.add))
            link(dve.tensor_scalar(spl[:, 0, :], acc, LRU_C, None, ALU.mult))
            dve.tensor_scalar(spl[:, 1, :], acc, -LRU_C, None, ALU.mult).then_inc(dve_step, 1)
            with dve.Fori(0, LC) as c:
                dve.wait_ge(lru_copied, 2 * c + 1)
                for tap in range(TAPS):
                    k = TAPS - 1 - tap
                    w_col = cols[:, bass.ds(c + C_CONVW + LC * k, 1)]
                    if tap == 0:
                        ins = dve.tensor_scalar(xc_t[:, c, :], u_t[:, c, :], w_col,
                                                cols[:, bass.ds(c + C_CONVB, 1)], ALU.mult, ALU.add)
                    else:
                        ins = dve.scalar_tensor_tensor(xc_t[:, c, tap:T], u_t[:, c, 0:T - tap], w_col,
                                                       xc_t[:, c, tap:T], ALU.mult, ALU.add)
                    if tap < TAPS - 1:
                        ins.then_inc(conv_step, 1)
                        dve.wait_ge(conv_step, 3 * c + tap + 1)
                    else:
                        ins.then_inc(conv_done, 1)
                lo(wl[0][:, :], wh[0][:, :], 0, 2 * c + 3)
                dve.wait_ge(xc_hi, c + 1)
                dve.tensor_tensor(gwl[:, :, :], gw_raw[:, c, :, :], gwh[:, :, :].bitcast(F32), ALU.subtract)
                dve.wait_ge(conv_done, c + 1)
                dve.tensor_tensor(xcl[:, :], xc_t[:, c, :], xch[:, :].bitcast(F32), ALU.subtract).then_inc(xc_lo, 1)
                dve.wait_ge(gelu_sq, c + 1)
                dve.tensor_scalar(lru_g[:, :], lru_g[:, :], GELU_A, 1.0, ALU.mult, ALU.add).then_inc(gelu_step, 1)
                dve.wait_ge(gelu_step, c + 1)
                dve.tensor_tensor(lru_g[:, :], lru_g[:, :], gel[:, c, :], ALU.mult).then_inc(gelu_in, 1)
                lo(wl[1][:, :], wh[1][:, :], 1, 2 * c + 4)
                dve.wait_ge(sig_done, 2 * c + 2)
                dve.tensor_tensor(xc_t[:, c, :], xc_t[:, c, :], lru_a[:, :], ALU.mult).then_inc(ix_done, 1)
                dve.wait_ge(gelu_sig, c + 1)
                dve.tensor_tensor(gel[:, c, :], gel[:, c, :], lru_g[:, :], ALU.mult).then_inc(gelu_done, 1)
            with dve.Fori(0, LC) as c:
                dve.wait_ge(decay_sq, c + 1)
                dve.wait_ge(tanh_done, LC)
                dve.scalar_tensor_tensor(u_t[:, c, :], lru_a[:, :], 1.0, u_t[:, c, :], ALU.add,
                                         ALU.mult).then_inc(bsq_done, 1)
            lo_early(P_V + 2)
            for first in (0, LC // 2):
                for c in range(first, first + LC // 2):
                    dve.wait_ge(sqrt_done, c + 1)
                    dve.wait_ge(ix_done, LC)
                    dve.tensor_tensor(xc_t[:, c, :], xc_t[:, c, :], u_t[:, c, :], ALU.mult).then_inc(scan_step, 1)
                    dve.wait_ge(scan_step, 2 * c + 1)
                    dve.tensor_tensor_scan(u_t[:, c, :], dec[:, c, :], xc_t[:, c, :], 0.0, ALU.mult,
                                           ALU.add).then_inc(scan_step, 1)
                    dve.wait_ge(scan_step, 2 * c + 2)
                    dve.wait_ge(gelu_done, LC)
                    dve.wait_ge(lru_spilled, 16 * c)
                    dve.tensor_tensor(lru_y[:, :], u_t[:, c, :], gel[:, c, :], ALU.mult).then_inc(lru_done, 1)
                if first == 0:
                    lo_early(P_V + 3)
            for t in range(TT):
                dve.wait_ge(v_hi, t + 1)
                dve.tensor_tensor(vl[:, t, :], bank(t), vh[:, t, :].bitcast(F32), ALU.subtract).then_inc(v_lo, 1)
            lo_early(P_QK)
            lo_early(P_QK + 1)
            dve.wait_ge(rope_loaded, 16)
            with dve.Fori(0, HEADS) as h:
                for s in range(2):
                    dve.wait_ge(q_copied, 2 * h + s + 1)
                    dve.wait_ge(rot_loaded, 128 * h + 64 * (s + 1))
                    dve.tensor_tensor(q_sb[:, s, :], q_sb[:, s, :], cos_t[:, 0, :], ALU.mult).then_inc(rope_step, 1)
                    dve.tensor_tensor(q_rot[:, :], q_rot[:, :], cos_t[:, 1, :], ALU.mult).then_inc(rope_step, 1)
                    lo(wl[s][:, :], wh[s][:, :], s, 2 * h + P_QK + s + 3)
                    dve.wait_ge(rope_step, 4 * h + 2 * s + 2)
                    dve.tensor_tensor(q_sb[:, s, :], q_sb[:, s, :], q_rot[:, :], ALU.add).then_inc(rope_sum, 1)
                    dve.wait_ge(rope_sum, 2 * h + s + 1)
                    dve.wait_ge(qk_hi, 2 * h + s + 1)
                    dve.scalar_tensor_tensor(yl[:, 2 * h + s, :], q_sb[:, s, :], Q_SCALE if s == 0 else 1.0,
                                             yh[:, 2 * h + s, :].bitcast(F32), ALU.mult,
                                             ALU.subtract).then_inc(qk_lo, 1)
            steps = TT * HEADS
            seen = [0]
            for s in range(steps + 1):
                if s >= 1:
                    p, i = s - 1, (s - 1) % TT
                    keys = slice(0, P * (i + 1))
                    dve.wait_ge(exped, 2 * p + 2)
                    link(dve.reciprocal(recip[:, :], denom[:, p % 2, :]))
                    link(dve.tensor_scalar(probs[:, p % 2, 1, keys], probs[:, p % 2, 1, keys], recip[:, 1:2],
                                           lam_e[:, 1:2], ALU.mult, ALU.mult))
                    dve.scalar_tensor_tensor(probs[:, p % 2, 0, keys], probs[:, p % 2, 0, keys], recip[:, 0:1],
                                             probs[:, p % 2, 1, keys], ALU.mult, ALU.add).then_inc(w_done, 1)
                if s < steps:
                    i = s % TT
                    for m in range(2):
                        dve.wait_ge(scores, 2 * s + m + 1)
                        dve.tensor_reduce(negmax[:, s % 2, m:m + 1], pair[m][:, 0:P * (i + 1)], AX.X, ALU.max,
                                          negate=True).then_inc(maxed, 1)
                if s >= 1:
                    p, i = s - 1, (s - 1) % TT
                    j = p // 2
                    th, tl = (xl[:, 0:2, :], xl[:, 2:4, :]) if j % 2 == 0 else (wt2h, wt2l)
                    if j % 2 == 0:
                        th = th.rearrange("p a (b q) -> p (a b) q", q=2 * P)
                        tl = tl.rearrange("p a (b q) -> p (a b) q", q=2 * P)
                    for b in range(i // 4 + 1):
                        dve.wait_ge(wt_hi, seen[0] + 1)
                        nb = min(4, i + 1 - 4 * b)
                        kq = (slice(None), slice(4 * b, 4 * b + nb), slice(P * (p % 2), P * (p % 2) + P))
                        dve.tensor_tensor(tl[kq], bank(4 + seen[0] % 2)[:, 0:P * nb].rearrange("p (k q) -> p k q", q=P),
                                          th[kq].bitcast(F32), ALU.subtract).then_inc(wt_lo, 1)
                        seen[0] += 1
            dve.wait_ge(sumsq_done, steps // 2)
            rsqrt_pre(bank(7)[:, 0:steps], hvar[:, :], P, head_var)
            dve.wait_ge(head_root, 1)
            rsqrt_post(hvar[:, :], hroot[:, :], ht1[:, :], ht2[:, :], hrstd[:, :])

            def diagonals(h):
                if h >= 2:
                    dve.wait_ge(spread_done, 2 * (h - 1))
                for t in range(TT):
                    ins = dve.tensor_scalar(diag[:, h % 2, P * t:P * t + P], ident[:, :],
                                            hrstd[:, TT * h + t:TT * h + t + 1], None, ALU.mult)
                ins.then_inc(diag_done, 1)

            diagonals(0)
            for h in range(HEADS):
                if h + 1 < HEADS:
                    diagonals(h + 1)
                dve.wait_ge(spread_done, 2 * h + 2)
                dve.scalar_tensor_tensor(o_raw[:, 2 * h, :], o_raw[:, 2 * h, :], head_gain[:, 0:1],
                                         pair[h % 2][:, :], ALU.mult, ALU.mult).then_inc(o_norm, 1)
                dve.wait_ge(o_norm, h + 1)
                dve.wait_ge(mix_hi, h + 1)
                dve.tensor_tensor(xl[:, LC + h, :], o_raw[:, 2 * h, :], xh[:, LC + h, :].bitcast(F32),
                                  ALU.subtract).then_inc(mix_lo, 1)
            for c in range(LC):
                dve.wait_ge(mix_hi, HEADS + c + 1)
                dve.tensor_tensor(xl[:, c, :], lru_raw[:, c, :], xh[:, c, :].bitcast(F32),
                                  ALU.subtract).then_inc(mix_lo, 1)
            for half in range(2):
                for j in range(2, 6):
                    lo_early(P_OUT + 4 * half + j)
            for t in range(TT):
                dve.wait_ge(y_copied, TT + t + 1)
                dve.wait_ge(y_squared, t)
                dve.tensor_tensor_reduce(out=junk2[:, :], in0=h_sb[:, t, :], in1=h_sb[:, t, :], scale=1.0, scalar=0.0,
                                         op0=ALU.mult, op1=ALU.add, accum_out=mean_sq[:, 1, t:t + 1]).then_inc(y_squared, 1)
            dve.wait_ge(y_squared, TT)
            dve.wait_ge(g_post_loaded, 16)
            for gq in range(2):
                sl = slice(4 * gq, 4 * gq + 4)
                rsqrt_pre(mean_sq[:, 1, sl], var[:, sl], D, post_var)
                dve.wait_ge(post_root, gq + 1)
                rsqrt_post(var[:, sl], root[:, sl], t1[:, sl], t2[:, sl], rstd[:, 1, sl])
                for t in range(4 * gq, 4 * gq + 4):
                    link(dve.scalar_tensor_tensor(h_sb[:, t, :], h_sb[:, t, :], rstd[:, 1, t:t + 1], g_post[:, :],
                                                  ALU.mult, ALU.mult))
                    dve.wait_ge(x_back[t % 2], 16 * (t // 2 + 1))
                    dve.tensor_tensor(h_sb[:, t, :], h_sb[:, t, :], x_re[:, t % 2, :], ALU.add).then_inc(h_done, 1)
                dve.wait_ge(h_squared, 4 * gq + 4)
                rsqrt_pre(mean_sq[:, 2, sl], var[:, sl], D, pre_var)
                dve.wait_ge(pre_root, gq + 1)
                rsqrt_post(var[:, sl], root[:, sl], t1[:, sl], t2[:, sl], rstd[:, 2, sl], pre_rstd)
            split_lo(16, yh, yl, C_GMLP)

            def act_unit(g, par, cc, hf):
                n = 4 * g + 2 * cc + hf
                dve.wait_ge(act_hi, n + 1)
                dve.tensor_tensor(relu[:, hf, :], relu[:, hf, :], relu[:, hf, :], ALU.mult).then_inc(relu_sq, 1)
                dve.wait_ge(relu_sq, n + 1)
                tok = slice(HALF * hf, HALF * hf + HALF)
                dve.tensor_tensor(xl[:, 2 * par + cc, tok], relu[:, hf, :], xh[:, 2 * par + cc, tok].bitcast(F32),
                                  ALU.subtract).then_inc(act_lo, 1)

            def sums(g):
                for t in range(TT):
                    dve.wait_ge(down_done, 8 * g + t + 1)
                    y = yacc[t // 4][:, t % 4, :]
                    dve.tensor_tensor(y, y, pair[2 + t % 2][:, :], ALU.add).then_inc(y_added, 1)

            def act_group(g, par, up_next):
                for cc in range(2):
                    act_unit(g, par, cc, 0)
                    act_unit(g, par, cc, 1)
                    if up_next:
                        lo(wl[cc][:, :], wh[cc][:, :], cc, 4 * g + P_UP + 2 + cc + 1)

            def down_lo(g, up_next):
                for cc in range(2):
                    lo(wdl[:, cc, :], wdh[:, cc, :], cc, 4 * g + P_UP + (4 if up_next else 2) + cc + 1)

            dve.wait_ge(acc_zero, 2)
            act_group(0, 0, True)
            down_lo(0, True)
            with dve.Fori(0, (GROUPS - 2) // 2) as i:
                for par in range(2):
                    g = 2 * i + par + 1
                    act_group(g, 1 - par, True)
                    sums(g - 1)
                    down_lo(g, True)
            act_group(GROUPS - 1, (GROUPS - 1) % 2, False)
            sums(GROUPS - 2)
            down_lo(GROUPS - 1, False)
            dve.wait_ge(g_out_loaded, 16)
            for t in range(TT):
                dve.wait_ge(down_done, 8 * (GROUPS - 1) + t + 1)
                y = yacc[t // 4][:, t % 4, :]
                dve.tensor_tensor(y, y, pair[2 + t % 2][:, :], ALU.add).then_inc(y_added, 1)
                dve.wait_ge(fin_sq, t + 1)
                c1 = slice(t, t + 1)
                rsqrt_pre(mean_sq[:, 3, c1], var[:, c1], D, fin_var)
                dve.wait_ge(fin_root, t + 1)
                rsqrt_post(var[:, c1], root[:, c1], t1[:, c1], t2[:, c1], rstd[:, 3, c1])
                link(dve.scalar_tensor_tensor(y, y, rstd[:, 3, c1], g_out[:, :], ALU.mult, ALU.mult))
                dve.tensor_tensor(h_sb[:, t, :], h_sb[:, t, :], y, ALU.add).then_inc(fin_done, 1)


def row_pieces(w, n_cols):
    r = D // n_cols
    w = w.reshape(-1, r, P, w.shape[1] // n_cols, n_cols)
    return w.transpose(3, 0, 2, 1, 4).reshape(-1, P, D)


def column_pieces(w):
    return w.reshape(KC, P, -1, P).transpose(2, 1, 0, 3).reshape(-1, P, D)


def lay_out_weights(w_in, w_out, w_up, w_down):
    u, g = column_pieces(w_in[:, :LRU]), column_pieces(w_in[:, LRU:2 * LRU])
    q = column_pieces(w_in[:, 2 * LRU:2 * LRU + HALF])
    k = column_pieces(w_in[:, 2 * LRU + HALF:2 * LRU + 2 * HALF])
    v = row_pieces(w_in[:, 2 * LRU + 2 * HALF:], HALF)
    up = column_pieces(w_up).reshape(GROUPS, 2, P, D)
    down = w_down.reshape(GROUPS, 2, P, D)
    parts = [np.stack([u, g], 1).reshape(-1, P, D), v, np.stack([q, k], 1).reshape(-1, P, D),
             row_pieces(w_out, HALF), up[0]]
    for n in range(GROUPS):
        if n + 1 < GROUPS:
            parts.append(up[n + 1])
        parts.append(down[n])
    return np.concatenate(parts)


def lay_out_gates(wa, wx):
    g = np.zeros((P, LC, 2, P), np.float32)
    for n, w in enumerate((wa, wx)):
        for c in range(LC):
            for b in range(2):
                g[64 * b:64 * b + 64, c, n, 64 * b:64 * b + 64] = w[2 * c + b]
    return g


def lay_out_columns(i):
    def col(v):
        return np.asarray(v).reshape(-1, P).T
    c = [col(i["norm_mix_pre"][0]), col(i["norm_mlp_pre"][0])]
    c += [col(i["conv_w"][0][k]) for k in range(TAPS)]
    c += [col(i["conv_b"][0]), col(i["b_gate_a"][0]), col(i["b_gate_x"][0]), col(i["lru_lambda"][0]),
          col(i["att_head_norm"][0])]
    return np.ascontiguousarray(np.concatenate(c, 1))


def rope_tables():
    half = np.float32(32)
    freqs = np.float32(10000.0) ** (-np.arange(32, dtype=np.float32) / half)
    ang = np.arange(T, dtype=np.float32)[:, None] * freqs[None, :]
    cos, sin = np.cos(ang).T, np.sin(ang).T
    return np.stack([np.concatenate([cos] * 4), np.concatenate([-sin, sin] * 2)], 1).astype(np.float32)


def kernel(**inputs):
    import concourse.bacc as bacc
    from concourse.bass_utils import run_bass_kernel_spmd

    i = {n: np.asarray(a) for n, a in inputs.items()}
    mask = np.where(np.arange(P)[None, :] > np.arange(P)[:, None], MASKED, 0.0)
    arrays = {
        "x": i["x"],
        "weights": lay_out_weights(i["w_in"][0], i["w_out"][0], i["w_up"][0], i["w_down"][0]),
        "gate_weights": lay_out_gates(i["w_gate_a"][0], i["w_gate_x"][0]),
        "columns": lay_out_columns(i),
        "lam_rows": np.stack([i[n][0] for n in ("lambda_q1", "lambda_k1", "lambda_q2", "lambda_k2")]),
        "post_gains": np.stack([i["norm_mix_post"][0], i["norm_mlp_post"][0]]),
        "rope": rope_tables(),
        "constants": np.stack([np.eye(P), mask]).astype(np.float32),
    }
    arrays = {n: np.ascontiguousarray(a) for n, a in arrays.items()}
    nc = bacc.Bacc("TRN2", target_bir_lowering=False, num_devices=1)
    args = [nc.dram_tensor(n, a.shape, mybir.dt.from_np(a.dtype), kind="ExternalInput").ap()
            for n, a in arrays.items()]
    spill = nc.dram_tensor("y_spill", (LC, P, T), F32, kind="Internal").ap()
    out = nc.dram_tensor("out", (1, T, D), F32, kind="ExternalOutput").ap()
    build(nc, *args, spill, out)
    return run_bass_kernel_spmd(nc, [arrays], core_ids=[0]).results[0]["out"]
```

```python
import math
from contextlib import ExitStack

import numpy as np

import concourse.bass as bass
from concourse import mybir

F32 = mybir.dt.float32
F32R = mybir.dt.float32r
ACT = mybir.ActivationFunctionType
ALU = mybir.AluOpType
AX = mybir.AxisListType

P = 128
D = 1024
T = 1024
KC = D // P
TT = T // P
HALF = 512
LRU = D // 2
LC = LRU // P
HEADS = 4
FF = 4 * D
TAPS = 4
EPS = 1e-6
LAM_INIT = 0.8 - 0.6 * math.exp(-0.3 * 0)
Q_SCALE = 64 ** -0.5
LRU_C = 8.0
GELU_A = 0.044715
GELU_S = 2.0 * math.sqrt(2.0 / math.pi)
MASKED = -1e30

N_LRU = 2 * LC
N_V = 4
N_QK = 2 * HEADS
N_OUT = 16
P_VA = N_LRU
P_QK = P_VA + N_V
P_VB = P_QK + N_QK
P_OUT = P_VB + N_V
P_UP = P_OUT + N_OUT
GROUPS = FF // (2 * P)
PIECES = P_UP + 4 * GROUPS

C_GPRE, C_GMLP = 0, KC
C_CONVW = 2 * KC
C_CONVB = C_CONVW + TAPS * LC
C_BA = C_CONVB + LC
C_BX = C_BA + LC
C_LAM = C_BX + LC
C_HEADG = C_LAM + LC
NCOLS = C_HEADG + 1


def build(nc, x, weights, gate_weights, columns, lam_rows, post_gains, rope, constants, y_spill, out):
    with ExitStack() as ctx:
        ctx.enter_context(nc.allow_non_contiguous_dma(reason="small parameters"))
        base = (nc.sbuf_base + 63) // 64 * 64
        KB = 1024

        at_x = base
        at_y = at_x + 64 * KB
        at_v = at_y + 64 * KB
        at_w = at_v + 32 * KB
        at_s = at_w + 24 * KB
        at_c = at_s + 20 * KB

        def sb(name, shape, dt, offset):
            return nc.alloc_sbuf_tensor_at(name, shape, dt, offset=offset)

        xh = sb("xh", [P, KC, T], F32R, at_x)
        xl = sb("xl", [P, KC, T], F32R, at_x + 32 * KB)
        probs = sb("probs", [P, 2, 2, T], F32, at_x)
        yacc = [sb("yacc0", [P, 4, D], F32, at_x + 16 * KB), sb("yacc1", [P, 4, D], F32, at_x + 48 * KB)]
        x_b = yacc[0]
        hm_b = yacc[1]
        yh = sb("yh", [P, KC, T], F32R, at_y)
        yl = sb("yl", [P, KC, T], F32R, at_y + 32 * KB)
        u_t = sb("u_t", [P, LC, T], F32, at_y)
        gel = sb("gel", [P, LC, T], F32, at_y + 16 * KB)
        xc_t = sb("xc_t", [P, LC, T], F32, at_y + 32 * KB)
        dec = sb("dec", [P, LC, T], F32, at_y + 48 * KB)
        o_raw = sb("o_raw", [P, KC, T], F32, at_y)
        lru_raw = sb("lru_raw", [P, LC, T], F32, at_y + 32 * KB)
        x_a = sb("x_a", [P, KC, T], F32, at_y)
        hm_a = sb("hm_a", [P, KC, T], F32, at_y + 32 * KB)
        x_sb = sb("x_sb", [P, TT, D], F32, at_v)
        vh = sb("vh", [P, TT, HALF], F32R, at_v)
        vl = sb("vl", [P, TT, HALF], F32R, at_v + 16 * KB)
        h_sb = sb("h_sb", [P, TT, D], F32, at_v)
        raw = [sb(f"raw{s}", [P, D], F32, at_w + 4 * s * KB) for s in range(2)]
        wh = [sb(f"wh{s}", [P, D], F32R, at_w + (8 + 4 * s) * KB) for s in range(2)]
        wl = [sb(f"wl{s}", [P, D], F32R, at_w + (16 + 4 * s) * KB) for s in range(2)]
        xch = sb("xch", [P, T], F32R, at_s)
        xcl = sb("xcl", [P, T], F32R, at_s + 4 * KB)
        lru_a = sb("lru_a", [P, T], F32, at_s + 8 * KB)
        lru_g = sb("lru_g", [P, T], F32, at_s + 12 * KB)
        gwh = sb("gwh", [P, 2, P], F32R, at_s + 16 * KB)
        gwl = sb("gwl", [P, 2, P], F32R, at_s + 17 * KB)
        cos_t = sb("cos_t", [P, 2, T], F32, at_s)
        q_sb = sb("q_sb", [P, 2, T], F32, at_s + 8 * KB)
        q_rot = sb("q_rot", [P, T], F32, at_s + 16 * KB)
        wt2h = sb("wt2h", [P, TT, 2 * P], F32R, at_s)
        wt2l = sb("wt2l", [P, TT, 2 * P], F32R, at_s + 8 * KB)
        o_sq = sb("o_sq", [P, 2, 2 * P], F32, at_s + 16 * KB)
        diag = sb("diag", [P, 2, T], F32, at_s)
        g_post = sb("g_post", [P, D], F32, at_s)
        junk = sb("junk", [P, 2, D], F32, at_s + 8 * KB)
        wdh = sb("wdh", [P, 2, D], F32R, at_s)
        wdl = sb("wdl", [P, 2, D], F32R, at_s + 8 * KB)
        relu = sb("relu", [P, 2, HALF], F32, at_s + 16 * KB)
        g_out = sb("g_out", [P, D], F32, at_w)
        out_junk = sb("out_junk", [P, D], F32, at_w + 4 * KB)

        small_at = [at_c]

        def small(name, shape, dt=F32):
            t = sb(name, shape, dt, small_at[0])
            n = 4
            for s in shape[1:]:
                n *= s
            small_at[0] += (n + 31) // 32 * 32
            assert small_at[0] <= nc.sbuf_usable_end
            return t

        ident = small("ident", [P, P])
        ident_r = small("ident_r", [P, P], F32R)
        mask_r = small("mask_r", [P, P], F32R)
        ones = small("ones", [P, P])
        cols = small("cols", [P, NCOLS])
        spl = small("spl", [P, 2, LC])
        tiny = small("tiny", [P, 6, LC])
        lam_e = small("lam_e", [P, 4])
        mean_sq = small("mean_sq", [P, 5, TT])
        var = small("var", [P, TT])
        root = small("root", [P, TT])
        t1 = small("t1", [P, TT])
        t2 = small("t2", [P, TT])
        rstd = small("rstd", [P, 4, TT])
        head_gain = small("head_gain", [P, 1])
        negmax = small("negmax", [P, 2, 2])
        sum0 = small("sum0", [P, 32])
        sum1 = small("sum1", [P, 2])
        blend = small("blend", [P, 2])
        sum0_eps = small("sum0_eps", [P, 32])
        hvar = small("hvar", [P, 32])
        hroot = small("hroot", [P, 32])
        ht1 = small("ht1", [P, 32])
        ht2 = small("ht2", [P, 32])
        hrstd = small("hrstd", [P, 32])
        gw_raw = sb("gw_raw", [P, LC, 2, P], F32, at_v)
        lam_raw = sb("lam_raw", [P, 4, 64], F32, at_s + 18 * KB)
        mask_raw = sb("mask_raw", [P, P], F32, at_s + 19 * KB)

        pair = [ctx.enter_context(nc.psum_tensor(f"pair{j}", [P, 2 * HALF], F32)) for j in range(4)]

        def bank(b):
            return pair[b // 2][:, HALF * (b % 2):HALF * (b % 2) + HALF]

        def score_bank(s, m):
            b = HALF * (s % 2) if s % TT < 4 else 0
            return pair[m][:, b:]

        def sem(name):
            return ctx.enter_context(nc.semaphore(name))

        x_loaded = [sem(f"x_loaded{i}") for i in range(4)]
        small_loaded = sem("small_loaded")
        ident_loaded = sem("ident_loaded")
        gates_loaded = sem("gates_loaded")
        raw_loaded = [sem(f"raw_loaded{s}") for s in range(2)]
        w_hi = sem("w_hi")
        w_lo = sem("w_lo")
        piece_used = sem("piece_used")
        const_ready = sem("const_ready")
        lam_step = sem("lam_step")
        act_step = sem("act_step")
        dve_step = sem("dve_step")
        dve_chain = sem("dve_chain")
        conv_step = sem("conv_step")
        gelu_step = sem("gelu_step")
        scan_step = sem("scan_step")
        rope_step = sem("rope_step")
        squares = sem("squares")
        squares_v = sem("squares_v")
        var_ready = sem("var_ready")
        root_ready = sem("root_ready")
        scaled = sem("scaled")
        tr_done = sem("tr_done")
        tr_hi = sem("tr_hi")
        tr_lo = sem("tr_lo")
        lru_copied = sem("lru_copied")
        conv_done = sem("conv_done")
        xc_hi = sem("xc_hi")
        xc_lo = sem("xc_lo")
        gates_done = sem("gates_done")
        sig_done = sem("sig_done")
        gelu_in = sem("gelu_in")
        gelu_sq = sem("gelu_sq")
        gelu_sig = sem("gelu_sig")
        gelu_done = sem("gelu_done")
        tanh_done = sem("tanh_done")
        ix_done = sem("ix_done")
        decay_done = sem("decay_done")
        decay_sq = sem("decay_sq")
        bsq_done = sem("bsq_done")
        sqrt_done = sem("sqrt_done")
        lru_done = sem("lru_done")
        lru_spilled = sem("lru_spilled")
        lru_back = sem("lru_back")
        v_hi = sem("v_hi")
        v_lo = sem("v_lo")
        rope_loaded = sem("rope_loaded")
        q_copied = sem("q_copied")
        rot_loaded = sem("rot_loaded")
        rope_sum = sem("rope_sum")
        qk_hi = sem("qk_hi")
        qk_lo = sem("qk_lo")
        scores = sem("scores")
        maxed = sem("maxed")
        exped = sem("exped")
        w_done = sem("w_done")
        wt_done = sem("wt_done")
        wt_hi = sem("wt_hi")
        wt_lo = sem("wt_lo")
        pv_done = sem("pv_done")
        o_copied = sem("o_copied")
        o_squared = sem("o_squared")
        sumsq_done = sem("sumsq_done")
        head_var = sem("head_var")
        head_root = sem("head_root")
        diag_done = sem("diag_done")
        spread_done = sem("spread_done")
        o_norm = sem("o_norm")
        mix_hi = sem("mix_hi")
        mix_lo = sem("mix_lo")
        lru_mixed = sem("lru_mixed")
        out_bank = sem("out_bank")
        y_copied = sem("y_copied")
        post_var = sem("post_var")
        post_root = sem("post_root")
        x_back = sem("x_back")
        y_scaled = sem("y_scaled")
        h_added = sem("h_added")
        g_post_loaded = sem("g_post_loaded")
        h_done = sem("h_done")
        h_squared = sem("h_squared")
        pre_var = sem("pre_var")
        pre_root = sem("pre_root")
        pre_rstd = sem("pre_rstd")
        hm_scaled = sem("hm_scaled")
        hm_scaled_v = sem("hm_scaled_v")
        acc_zero = sem("acc_zero")
        up_done = sem("up_done")
        relu_done = sem("relu_done")
        act_hi = sem("act_hi")
        relu_sq = sem("relu_sq")
        act_lo = sem("act_lo")
        down_done = sem("down_done")
        y_added = sem("y_added")
        fin_sq = sem("fin_sq")
        fin_var = sem("fin_var")
        fin_root = sem("fin_root")
        g_out_loaded = sem("g_out_loaded")
        fin_scaled = sem("fin_scaled")
        fin_done = sem("fin_done")
        stored = sem("stored")

        block = ctx.enter_context(nc.Block())

        def mm3(pe, o, a_hi, a_lo, b_hi, b_lo, first, last):
            pe.matmul(o, a_hi, b_hi, start=first, stop=False)
            pe.matmul(o, a_hi, b_lo, start=False, stop=False)
            return pe.matmul(o, a_lo, b_hi, start=False, stop=last)

        def groups_upto(s):
            return sum(n % TT // 4 + 1 for n in range(s + 1))

        def last_pair(t):
            return (2 + t) % 4

        w_banks = (4, 5, 7)
        head_sums = bank(6)[:, 2 * P:2 * P + TT * HEADS]

        lru_mix = [21, 23, 25, 27]

        final = [(0, 1), (2, 3), (4, 5), (6,), (7,)]

        def used(p):
            def is_last(n):
                return (P_VA <= n < P_QK or n >= P_VB) and (n - P_VA) % 4 == 3
            quarters = sum(is_last(n) for n in range(p + 1))
            return (out_bank, 4 * quarters) if is_last(p) else (piece_used, p + 1 - quarters)

        def mixed_slot(k):
            return (k + LC) % KC

        def halves(ap):
            return ap.rearrange("p (a b) -> p a b", b=HALF)

        def tile_a(t_, t):
            return t_[:, 2 * t:2 * t + 2, HALF:T]

        def pieces_of(t):
            return t[:, :].rearrange("p (k c) -> p k c", c=P)

        @block.sync
        def _(sp):
            for i in range(4):
                sp.dma_start(x_sb[:, 2 * i:2 * i + 2, :],
                             x[0].rearrange("(t p) d -> p t d", p=P)[:, 2 * i:2 * i + 2, :]).then_inc(x_loaded[i], 16)
            for s in range(2):
                sp.dma_start(raw[s][:, :], weights[s]).then_inc(raw_loaded[s], 16)
            with sp.Fori(0, PIECES // 2 - 1) as i:
                for s in range(2):
                    sp.wait_ge(w_lo, 2 * i + s + 1)
                    sp.dma_start(raw[s][:, :], weights[2 * i + s + 2]).then_inc(raw_loaded[s], 16)
            sp.wait_ge(w_lo, PIECES)
            sp.dma_start(g_out[:, :], post_gains[1].partition_broadcast(P)).then_inc(g_out_loaded, 16)
            for t in range(TT):
                sp.wait_ge(fin_done, t + 1)
                sp.dma_start(out[0, P * t:P * t + P, :], h_sb[:, t, :]).then_inc(stored, 16)
            sp.wait_ge(stored, 16 * TT)

        @block.gpsimd
        def _(pool):
            pool.dma_start(mask_raw[:, :], constants[1]).then_inc(small_loaded, 16)
            pool.dma_start(lam_raw[:, :, :], lam_rows.partition_broadcast(P)).then_inc(small_loaded, 16)
            pool.wait_ge(tr_done, 16)
            pool.dma_start(gw_raw[:, :, :, :], gate_weights).then_inc(gates_loaded, 16)
            for c in range(LC):
                pool.wait_ge(lru_done, c + 1)
                pool.dma_start(y_spill[c], gel[:, c, :]).then_inc(lru_spilled, 16)
            pool.dma_start(cos_t[:, :, :], rope).then_inc(rope_loaded, 16)
            pool.wait_ge(lru_spilled, 16 * LC)
            pool.wait_ge(scores, 2 * TT * HEADS // 2)
            pool.dma_start(lru_raw[:, :, :], y_spill.rearrange("c p t -> p c t")).then_inc(lru_back, 16)
            for c in range(LC):
                pool.wait_ge(mix_hi, c + 1)
                nc.gpsimd.tensor_tensor(xl[:, LC + c, :], lru_raw[:, c, :], xh[:, LC + c, :].bitcast(F32),
                                        ALU.subtract).then_inc(lru_mixed, 1)
            pool.wait_ge(spread_done, 2 * HEADS)
            pool.dma_start(g_post[:, :], post_gains[0].partition_broadcast(P)).then_inc(g_post_loaded, 16)
            pool.wait_ge(mix_lo, HEADS)
            for t in range(TT // 2):
                pool.dma_start(tile_a(x_a, t), halves(x[0, P * t:P * t + P, :])).then_inc(x_back, 16)
            for half in range(2):
                if half == 1:
                    pool.wait_ge(out_bank, 3 * TT)
                    pool.dma_start(x_b[:, :, :], x[0, T // 2:T, :].rearrange("(t p) d -> p t d", p=P)
                                   ).then_inc(x_back, 16)
                for t in range(2):
                    pool.wait_ge(y_scaled, 4 * half + t + 1)
                    pool.wait_ge(x_back, 16 * (4 + half))
                    hv = halves(h_sb[:, 4 * half + t, :])
                    xv = halves(x_b[:, t, :]) if half else tile_a(x_a, t)
                    nc.gpsimd.tensor_tensor(hv, hv, xv, ALU.add).then_inc(h_added, 1)
            pool.wait_ge(h_done, 4)
            pool.wait_ge(h_added, 4)
            nc.gpsimd.memset(yacc[0][:, :, :], 0.0).then_inc(acc_zero, 1)
            pool.wait_ge(tr_done, 32)
            nc.gpsimd.memset(yacc[1][:, :, :], 0.0).then_inc(acc_zero, 1)
            for t in range(TT):
                pool.wait_ge(fin_scaled, t + 1)
                nc.gpsimd.tensor_tensor(h_sb[:, t, :], h_sb[:, t, :], yacc[t // 4][:, t % 4, :],
                                        ALU.add).then_inc(fin_done, 1)

        @block.tensor
        def _(pe):
            def transposes(tiles, b):
                for t in range(4):
                    mm = pe.transpose(bank(b)[:, P * t:P * t + P], tiles[t], ident[:, :])
                mm.then_inc(tr_done, 1)

            def feature_bank(slot, o, rh, rl, hf, split_from=None):
                tok = slice(HALF * hf, HALF * hf + HALF)
                for k in range(KC):
                    if split_from is not None:
                        pe.wait_ge(tr_lo, split_from + k + 1)
                    mm = mm3(pe, o, pieces_of(wh[slot])[:, k, :], pieces_of(wl[slot])[:, k, :],
                             rh[:, k, tok], rl[:, k, tok], k == 0, k == KC - 1)
                return mm

            def feature_piece(slot, out_pair, rh, rl):
                for hf in range(2):
                    yield feature_bank(slot, out_pair[:, HALF * hf:HALF * hf + HALF], rh, rl, hf)

            def token_piece(slot, j, tiles, bank0, copied=None, chunk=lambda k: k):
                for kk in range(2):
                    k = 2 * j + kk
                    w_cols = slice(HALF * kk, HALF * kk + HALF)
                    for n, t in enumerate(tiles):
                        tok = slice(P * t, P * t + P)
                        if k == 0 and copied is not None:
                            pe.wait_ge(copied[0], copied[1] + n + 1)
                        mm = mm3(pe, bank(bank0 + n), xh[:, chunk(k), tok], xl[:, chunk(k), tok], wh[slot][:, w_cols],
                                 wl[slot][:, w_cols], k == 0, k == KC - 1)
                        if k == KC - 1:
                            mm.then_inc(out_bank, 1)
                if j < KC // 2 - 1:
                    mm.then_inc(piece_used, 1)

            pe.wait_ge(ident_loaded, 32)
            for hf in range(2):
                pe.wait_ge(scaled, 4 * (hf + 1))
                for k in range(KC):
                    if hf == 1:
                        pe.wait_ge(tr_lo, k + 1)
                    transposes([x_sb[:, 4 * hf + t, P * k:P * k + P] for t in range(4)], k)
            with pe.Fori(0, LC) as c:
                for s in range(2):
                    pe.wait_ge(w_lo, 2 * c + s + 1)
                    if s == 0:
                        pe.wait_ge(tr_lo, KC + 1)
                    for hf in range(2):
                        if s == 0 and hf == 1:
                            pe.wait_ge(tr_lo, 2 * KC)
                        mm = feature_bank(s, pair[s][:, HALF * hf:HALF * hf + HALF], xh, xl, hf)
                    mm.then_inc(piece_used, 1)
                pe.wait_ge(xc_lo, c + 1)
                for g in range(2):
                    for hf in range(2):
                        tok = slice(HALF * hf, HALF * hf + HALF)
                        mm = mm3(pe, pair[2 + g][:, tok], gwh[:, g, :], gwl[:, g, :], xch[:, tok],
                                 xcl[:, tok], True, True)
                    mm.then_inc(gates_done, 1)
            pe.wait_ge(lru_copied, 2 * LC)
            pe.wait_ge(sig_done, 2 * LC)
            for j in range(N_V):
                pe.wait_ge(w_lo, P_VA + j + 1)
                token_piece(j % 2, j, range(4), 4)
            with pe.Fori(0, HEADS) as h:
                for s in range(2):
                    pe.wait_ge(w_lo, 2 * h + P_QK + s + 1)
                    for mm in feature_piece(s, pair[s], xh, xl):
                        pass
                    mm.then_inc(piece_used, 1)
            for j in range(N_V):
                pe.wait_ge(w_lo, P_VB + j + 1)
                token_piece(j % 2, j, range(4, TT), 4, (v_lo, 0))
            pe.wait_ge(const_ready, 1)
            pe.wait_ge(act_step, 1)
            groups_before = [0]

            def score_step(s):
                h, i = divmod(s, TT)
                if i == 0:
                    pe.wait_ge(qk_lo, 2 * (h + 1))
                q_tok = slice(P * i, P * i + P)
                for m in range(2):
                    rows = slice(64 * m, 64 * m + 64)
                    if s == 0:
                        pe.wait_ge(q_copied, 2 * HEADS)
                    elif s >= 2 and 1 <= i < 4:
                        pe.wait_ge(exped, 2 * (s - 2) + m + 1)
                    elif s >= 2 or i >= 4:
                        pe.wait_ge(exped, 2 * (s - 1) + m + 1)
                    n_banks = i // 4 + 1
                    for b in range(n_banks):
                        k_hi = min(P * (i + 1), HALF * (b + 1))
                        keys = slice(HALF * b, k_hi)
                        last = b == n_banks - 1
                        mm = mm3(pe, score_bank(s, m)[:, keys], yh[rows, 2 * h, q_tok], yl[rows, 2 * h, q_tok],
                                 yh[rows, 2 * h + 1, keys], yl[rows, 2 * h + 1, keys], True, not last)
                        if last:
                            mm = pe.matmul(score_bank(s, m)[:, P * i:P * i + P], ident_r[:, :], mask_r[:, :],
                                           start=False, stop=True)
                    mm.then_inc(scores, 1)

            def transpose_step(s):
                i = s % TT
                pe.wait_ge(w_done, s + 1)
                for b in range(i // 4 + 1):
                    g = groups_before[0]
                    if g >= 3:
                        pe.wait_ge(wt_lo, g - 2)
                    for kb in range(4 * b, min(4 * b + 4, i + 1)):
                        mm = pe.transpose(bank(w_banks[g % 3])[:, P * (kb - 4 * b):P * (kb - 4 * b) + P],
                                          probs[:, s % 2, 0, P * kb:P * kb + P], ident[:, :])
                    mm.then_inc(wt_done, 1)
                    groups_before[0] += 1

            def pv_step(j):
                h, jj = divmod(j, TT // 2)
                pe.wait_ge(wt_lo, groups_upto(2 * j + 1))
                if j >= 1:
                    pe.wait_ge(o_copied, j)
                th, tl = (xl[:, 0:2, :], xl[:, 2:4, :]) if j % 2 == 0 else (wt2h, wt2l)
                if j % 2 == 0:
                    th = th.rearrange("p a (b q) -> p (a b) q", q=2 * P)
                    tl = tl.rearrange("p a (b q) -> p (a b) q", q=2 * P)
                n = 2 * jj + 2
                e = slice(P * h, P * h + P)
                for kb in range(n):
                    q0 = P if kb == n - 1 else 0
                    mm = mm3(pe, bank(6)[:, q0:2 * P], vh[:, kb, e], vl[:, kb, e], th[:, kb, q0:],
                             tl[:, kb, q0:], kb == 0, kb == n - 1)
                mm.then_inc(pv_done, 1)

            def sumsq_step(j):
                pe.wait_ge(o_squared, j + 1)
                for i in range(2):
                    col = 2 * j + i
                    mm = pe.matmul(head_sums[:, col:col + 1], o_sq[:, j % 2, P * i:P * i + P], ones[:, 0:1],
                                   start=True, stop=True)
                mm.then_inc(sumsq_done, 1)

            steps = TT * HEADS
            for s in range(steps + 1):
                if s < steps:
                    score_step(s)
                if s % 2 == 0 and s >= 4:
                    if s >= 6:
                        sumsq_step(s // 2 - 3)
                    pv_step(s // 2 - 2)
                if s >= 1:
                    if s == 1:
                        pe.wait_ge(v_lo, TT)
                    transpose_step(s - 1)
            sumsq_step(steps // 2 - 2)
            pv_step(steps // 2 - 1)
            sumsq_step(steps // 2 - 1)
            def spread(h):
                pe.wait_ge(diag_done, h + 1)
                if h >= 2:
                    pe.wait_ge(o_norm, h - 1)
                for hf in range(2):
                    mm = pe.matmul(pair[2 + h % 2][:, HALF * hf:HALF * hf + HALF], ones[:, :],
                                   diag[:, h % 2, HALF * hf:HALF * hf + HALF], start=True, stop=True)
                    mm.then_inc(spread_done, 1)


            def hm_transposes(half, k):
                if half == 0:
                    tiles = [hm_a[:, 2 * t + k // 4, HALF + P * (k % 4):HALF + P * (k % 4) + P] for t in range(4)]
                else:
                    tiles = [hm_b[:, t, P * k:P * k + P] for t in range(4)]
                if k < 4:
                    pe.wait_ge(y_copied, 12 + 4 * half)
                else:
                    pe.wait_ge(tr_lo, 16 + 8 * half + k - 3)
                transposes(tiles, 4 * half + k % 4)

            for quarter in range(4):
                for j in range(4):
                    pe.wait_ge(w_lo, P_OUT + 4 * quarter + j + 1)
                    if quarter == 0:
                        if j < 2:
                            pe.wait_ge(lru_mixed, LC)
                        else:
                            pe.wait_ge(mix_lo, 2 * j - 2)
                        if j == 1:
                            spread(0)
                            spread(1)
                        if j == 2:
                            spread(2)
                            spread(3)
                    if quarter == 3 and j >= 2:
                        pe.wait_ge(hm_scaled, 4)
                        for k in range(4 * (j - 2), 4 * (j - 2) + 4):
                            hm_transposes(0, k)
                    token_piece(j % 2, j, range(4 * (quarter // 2), 4 * (quarter // 2) + 4), 4 * (quarter % 2),
                                (y_copied, 4 * quarter - 8) if quarter >= 2 else None, mixed_slot)

            def up(g2):
                for cc in range(2):
                    pe.wait_ge(w_lo, 2 * g2 + (P_UP - 2) + cc + 1)
                    for mm in feature_piece(cc, pair[cc], yh, yl):
                        mm.then_inc(up_done, 1)

            def up_waits(g2):
                pe.wait_ge(relu_done, 2 * g2)

            def down(g, par, wait_piece, last=False):
                pe.wait_ge(act_lo, 4 * g + 4)
                pe.wait_ge(w_lo, wait_piece)
                for t in range(TT):
                    if last and t >= 2:
                        if t >= 4:
                            pe.wait_ge(y_added, 8 * g + t - 3)
                    elif t >= 2:
                        pe.wait_ge(y_added, 8 * g + t - 1)
                    elif not (isinstance(g, int) and g == 0):
                        pe.wait_ge(y_added, 8 * g + t - 1)
                    tok = slice(P * t, P * t + P)
                    for hf in range(2):
                        o = pair[last_pair(t) if last else 2 + t % 2][:, HALF * hf:HALF * hf + HALF]
                        for cc in range(2):
                            a = 2 * par + cc
                            mm = mm3(pe, o, xh[:, a, tok], xl[:, a, tok],
                                     wdh[:, cc, HALF * hf:HALF * hf + HALF],
                                     wdl[:, cc, HALF * hf:HALF * hf + HALF], cc == 0, cc == 1)
                    mm.then_inc(down_done, 1)

            for cc in range(2):
                pe.wait_ge(w_lo, P_UP + cc + 1)
                feature_bank(cc, bank(2 * cc), yh, yl, 0, 16).then_inc(up_done, 1)
            pe.wait_ge(hm_scaled, 6)
            pe.wait_ge(hm_scaled_v, 2)
            for k in range(KC):
                hm_transposes(1, k)
            for cc in range(2):
                feature_bank(cc, bank(2 * cc + 1), yh, yl, 1, 24).then_inc(up_done, 1)
            up_waits(2)
            up(2)
            down(0, 0, P_UP + 6)
            with pe.Fori(0, (GROUPS - 2) // 2) as i:
                for par in range(2):
                    g = 2 * i + par + 1
                    up_waits(2 * g + 2)
                    up(2 * g + 2)
                    down(g, 1 - par, 4 * g + P_UP + 6)
            down(GROUPS - 1, (GROUPS - 1) % 2, PIECES, last=True)

        @block.scalar
        def _(act):
            def hi(p, dst, slot_wait=None):
                s = slot_wait[2]
                act.wait_ge(raw_loaded[s], slot_wait[3])
                if slot_wait[0] is not None:
                    act.wait_ge(slot_wait[0], slot_wait[1])
                act.activation(dst, raw[s][:, :], ACT.Copy).then_inc(w_hi, 1)

            def hi_early(p):
                free = (None, None) if p < 2 else used(p - 2)
                hi(p, wh[p % 2][:, :], (*free, p % 2, 16 * (p // 2 + 1)))

            act.dma_start(ident[:, :], constants[0]).then_inc(ident_loaded, 16)
            act.dma_start(cols[:, :], columns).then_inc(ident_loaded, 16)
            n_sq = 0
            for t in range(TT):
                if t % 4 < 3:
                    if t % 2 == 0:
                        act.wait_ge(x_loaded[t // 2], 16)
                    if n_sq >= 2:
                        act.wait_ge(squares, n_sq - 1)
                    act.activation(u_t[:, n_sq % 2, :], x_sb[:, t, :], ACT.Square,
                                   accum_out=mean_sq[:, 0, t:t + 1]).then_inc(squares, 1)
                    n_sq += 1
                else:
                    act.wait_ge(var_ready, t // 4 + 1)
                    act.activation(root[:, t - 3:t + 1], var[:, t - 3:t + 1], ACT.Sqrt).then_inc(root_ready, 1)
            hi_early(0)
            act.wait_ge(ident_loaded, 32)

            def split_hi(n, dst, gain0, b):
                hf, k = divmod(n % 16, KC)
                act.wait_ge(tr_done, n + 1)
                act.activation(dst[:, k, HALF * hf:HALF * hf + HALF], bank(b), ACT.Copy,
                               scale=cols[:, gain0 + k:gain0 + k + 1]).then_inc(tr_hi, 1)

            for n in range(2 * KC):
                split_hi(n, xh, C_GPRE, n % KC)
            hi_early(1)
            act.wait_ge(small_loaded, 32)
            act.activation(ident_r[:, :], ident[:, :], ACT.Copy)
            act.activation(mask_r[:, :], mask_raw[:, :], ACT.Copy).then_inc(act_step, 1)
            act.wait_ge(lam_step, 1)
            act.activation(lam_e[:, 2:4], lam_e[:, 0:2], ACT.Exp)
            act.activation(tiny[:, 1, :], tiny[:, 0, :], ACT.Exp, scale=-1.0).then_inc(act_step, 1)
            act.wait_ge(gates_loaded, 16)
            act.wait_ge(dve_step, 1)
            for c in range(LC):
                act.wait_ge(piece_used, 2 * c + 1)
                act.activation(u_t[:, c, :], pair[0][:, :], ACT.Copy).then_inc(lru_copied, 1)
                hi(None, wh[0][:, :], (piece_used, 2 * c + 1, 0, 16 * c + 32))
                act.wait_ge(conv_done, c + 1)
                act.activation(gwh[:, :, :], gw_raw[:, c, :, :], ACT.Copy)
                act.activation(xch[:, :], xc_t[:, c, :], ACT.Copy).then_inc(xc_hi, 1)
                act.wait_ge(piece_used, 2 * c + 2)
                act.activation(gel[:, c, :], pair[1][:, :], ACT.Copy).then_inc(lru_copied, 1)
                act.wait_ge(lru_copied, 2 * c + 2)
                act.wait_ge(gelu_done, c)
                act.activation(lru_g[:, :], gel[:, c, :], ACT.Square).then_inc(gelu_sq, 1)
                hi(None, wh[1][:, :], (piece_used, 2 * c + 2, 1, 16 * c + 32))
                act.wait_ge(gates_done, 2 * c + 1)
                act.activation(dec[:, c, :], pair[2][:, :], ACT.Sigmoid,
                               bias=cols[:, bass.ds(c + C_BA, 1)]).then_inc(sig_done, 1)
                act.wait_ge(gates_done, 2 * c + 2)
                act.wait_ge(ix_done, c)
                act.activation(lru_a[:, :], pair[3][:, :], ACT.Sigmoid,
                               bias=cols[:, bass.ds(c + C_BX, 1)]).then_inc(sig_done, 1)
                act.wait_ge(gelu_in, c + 1)
                act.activation(lru_g[:, :], lru_g[:, :], ACT.Sigmoid, scale=GELU_S).then_inc(gelu_sig, 1)
                act.wait_ge(sig_done, 2 * c + 2)
                act.activation(u_t[:, c, :], dec[:, c, :], ACT.Tanh,
                               scale=spl[:, 0, bass.ds(c, 1)]).then_inc(tanh_done, 1)
            act.wait_ge(tanh_done, LC)
            for c in range(LC):
                act.activation(dec[:, c, :], dec[:, c, :], ACT.Exp,
                               scale=spl[:, 1, bass.ds(c, 1)]).then_inc(decay_done, 1)
                act.wait_ge(decay_done, c + 1)
                act.wait_ge(bsq_done, c)
                act.wait_ge(ix_done, LC)
                act.activation(lru_a[:, :], dec[:, c, :], ACT.Square).then_inc(decay_sq, 1)
                if c == 1:
                    hi_early(P_VA + 2)
            act.wait_ge(bsq_done, LC)
            for c in range(LC):
                if c == LC // 2:
                    hi_early(P_VA + 3)
                act.activation(u_t[:, c, :], u_t[:, c, :], ACT.Sqrt).then_inc(sqrt_done, 1)

            def v_copies(half):
                for t in range(4 * half, 4 * half + 4):
                    act.wait_ge(out_bank, t + 1)
                    act.activation(vh[:, t, :], bank(4 + t % 4), ACT.Copy).then_inc(v_hi, 1)

            hi_early(P_QK)
            v_copies(0)
            hi_early(P_QK + 1)
            act.wait_ge(lru_spilled, 16 * LC)
            for h in range(HEADS):
                for s in range(2):
                    act.wait_ge(piece_used, 2 * h + P_QK + s)
                    act.wait_ge(rope_loaded, 16)
                    act.wait_ge(qk_lo, 2 * h)
                    act.activation(q_sb[:, s, :], pair[s][:, :], ACT.Copy).then_inc(q_copied, 1)
                    hi(None, wh[s][:, :], (piece_used, 2 * h + P_QK + s, s, 16 * h + 16 * (P_QK // 2 + 2)))
                    act.wait_ge(q_copied, 2 * h + s + 1)
                    if s == 1:
                        act.wait_ge(rope_sum, 2 * h + 1)
                    for m in range(2):
                        a, b = 64 * m, 64 * m + 32
                        act.dma_start(q_rot[a:a + 32, :], q_sb[b:b + 32, s, :]).then_inc(rot_loaded, 16)
                        act.dma_start(q_rot[b:b + 32, :], q_sb[a:a + 32, s, :]).then_inc(rot_loaded, 16)
                    act.wait_ge(rope_sum, 2 * h + s + 1)
                    act.activation(yh[:, 2 * h + s, :], q_sb[:, s, :], ACT.Copy,
                                   scale=Q_SCALE if s == 0 else 1.0).then_inc(qk_hi, 1)
            hi_early(P_VB + 2)
            hi_early(P_VB + 3)
            hi_early(P_OUT)
            v_copies(1)
            steps = TT * HEADS
            seen = [0]

            def exp_step(s):
                i = s % TT
                for m in range(2):
                    act.wait_ge(maxed, 2 * s + m + 1)
                    if s >= 2:
                        act.wait_ge(wt_done, groups_upto(s - 2))
                    act.activation(probs[:, s % 2, m, 0:P * (i + 1)], score_bank(s, m)[:, 0:P * (i + 1)], ACT.Exp,
                                   bias=negmax[:, s % 2, m:m + 1],
                                   accum_out=sum1[:, s % 2:s % 2 + 1] if m else sum0[:, s:s + 1]
                                   ).then_inc(exped, 1)

            def wt_hi_step(p):
                i, j = p % TT, p // 2
                th = xl[:, 0:2, :].rearrange("p a (b q) -> p (a b) q", q=2 * P) if j % 2 == 0 else wt2h
                for b in range(i // 4 + 1):
                    act.wait_ge(wt_done, seen[0] + 1)
                    if j >= 2:
                        act.wait_ge(pv_done, j - 1)
                    nb = min(4, i + 1 - 4 * b)
                    act.activation(th[:, 4 * b:4 * b + nb, P * (p % 2):P * (p % 2) + P],
                                   bank(w_banks[seen[0] % 3])[:, 0:P * nb].rearrange("p (k q) -> p k q", q=P),
                                   ACT.Copy).then_inc(wt_hi, 1)
                    seen[0] += 1

            def o_step(j):
                h, jj = divmod(j, TT // 2)
                q = slice(2 * P * jj, 2 * P * jj + 2 * P)
                act.wait_ge(pv_done, j + 1)
                act.activation(o_raw[:, 2 * h, q], bank(6)[:, 0:2 * P], ACT.Copy).then_inc(o_copied, 1)
                act.wait_ge(o_copied, j + 1)
                if j >= 2:
                    act.wait_ge(sumsq_done, j - 1)
                act.activation(o_sq[:, j % 2, :], o_raw[:, 2 * h, q], ACT.Square).then_inc(o_squared, 1)

            for s in range(steps + 1):
                if s < steps:
                    exp_step(s)
                if s % 2 == 0 and s >= 4:
                    o_step(s // 2 - 2)
                if s >= 1:
                    wt_hi_step(s - 1)
                if s == 5:
                    hi_early(P_OUT + 1)
                if s in lru_mix:
                    c = lru_mix.index(s)
                    act.wait_ge(lru_back, 16)
                    act.activation(xh[:, LC + c, :], lru_raw[:, c, :], ACT.Copy).then_inc(mix_hi, 1)
            o_step(steps // 2 - 1)
            act.wait_ge(head_var, 1)
            act.activation(hroot[:, :], hvar[:, :], ACT.Sqrt).then_inc(head_root, 1)
            for h in range(HEADS):
                if h % 2 == 0:
                    hi_early(P_OUT + 2 + h // 2)
                act.wait_ge(o_norm, h + 1)
                act.activation(xh[:, h, :], o_raw[:, 2 * h, :], ACT.Copy).then_inc(mix_hi, 1)
            def roots(half, var_sem, root_sem):
                sl = slice(4 * half, 4 * half + 4)
                act.wait_ge(var_sem, half + 1)
                act.activation(root[:, sl], var[:, sl], ACT.Sqrt).then_inc(root_sem, 1)

            def copies(quarter):
                cols_ = slice(HALF * (quarter % 2), HALF * (quarter % 2) + HALF)
                for n in range(4):
                    t = 4 * (quarter // 2) + n
                    o = bank(4 * (quarter % 2) + n)
                    done = 4 * quarter + n
                    act.wait_ge(out_bank, TT + done + 1)
                    act.activation(h_sb[:, t, cols_], o, ACT.Copy)
                    if done >= 2:
                        act.wait_ge(y_copied, done - 1)
                    act.activation(junk[:, done % 2, 0:HALF], o, ACT.Square,
                                   accum_out=mean_sq[:, 4 if quarter % 2 else 1, t:t + 1]).then_inc(y_copied, 1)

            def h_squares(half, tiles):
                for t in tiles:
                    n = 4 * half + t
                    if t < 2:
                        act.wait_ge(h_added, 2 * half + t + 1)
                    else:
                        act.wait_ge(h_done, 2 * half + t - 1)
                    if n >= 2:
                        act.wait_ge(h_squared, n - 1)
                    act.wait_ge(y_copied, 8 * half + 8)
                    act.activation(junk[:, n % 2, :], h_sb[:, n, :], ACT.Square,
                                   accum_out=mean_sq[:, 2, n:n + 1]).then_inc(h_squared, 1)

            def hm_tiles(half):
                act.wait_ge(pre_rstd, half + 1)
                for t in range(2 if half else 4):
                    act.activation(halves(hm_b[:, t, :]) if half else tile_a(hm_a, t),
                                   halves(h_sb[:, 4 * half + t, :]), ACT.Copy,
                                   scale=rstd[:, 2, 4 * half + t:4 * half + t + 1]).then_inc(hm_scaled, 1)

            for quarter in range(2):
                p = P_OUT + 4 * quarter
                for j in range(4 if quarter == 0 else 2, 6):
                    hi_early(p + j)
                copies(quarter)
            p = P_OUT + 8
            hi_early(p + 2)
            roots(0, post_var, post_root)
            hi_early(p + 3)
            h_squares(0, (0, 1))
            hi_early(p + 4)
            h_squares(0, (2, 3))
            roots(0, pre_var, pre_root)
            hm_tiles(0)
            hi_early(p + 5)
            copies(2)
            p = P_OUT + 12
            hi_early(p + 2)
            for k in range(4):
                split_hi(16 + k, yh, C_GMLP, k)
            hi_early(p + 3)
            for k in range(4, KC):
                split_hi(16 + k, yh, C_GMLP, k % 4)
            hi_early(p + 4)
            copies(3)
            roots(1, post_var, post_root)
            hi_early(p + 5)
            h_squares(1, range(4))
            roots(1, pre_var, pre_root)
            hm_tiles(1)
            for k in range(KC):
                split_hi(24 + k, yh, C_GMLP, 4 + k % 4)

            def act_unit(g, par, cc, hf):
                first = isinstance(g, int) and g == 0
                n, slot = (2 * hf + cc, cc) if first else (4 * g + 2 * cc + hf, hf)
                act.wait_ge(up_done, n + 1)
                if not (first and hf == 0):
                    act.wait_ge(act_lo, n - 1)
                act.activation(relu[:, slot, :], bank(2 * cc + hf), ACT.Relu).then_inc(relu_done, 1)
                act.wait_ge(relu_done, n + 1)
                act.activation(xh[:, 2 * par + cc, HALF * hf:HALF * hf + HALF], relu[:, slot, :],
                               ACT.Square).then_inc(act_hi, 1)

            def act_group(g, par, up_next, down_next):
                for cc in range(2):
                    act_unit(g, par, cc, 0)
                    act_unit(g, par, cc, 1)
                    if up_next:
                        hi(None, wh[cc][:, :], (up_done, 4 * g + 2 * cc + 2, cc, 32 * g + 16 * (P_UP // 2 + 2)))
                for cc in range(2):
                    late = 2 if up_next else 0
                    w = (None, None) if isinstance(g, int) and g == 0 else (down_done, 8 * g)
                    hi(None, wdh[:, cc, :], (*w, cc, 32 * g + 16 * (P_UP // 2 + 2 + late // 2)))

            for hf in range(2):
                for cc in range(2):
                    act_unit(0, 0, cc, hf)
            act.wait_ge(h_squared, TT)
            for cc in range(2):
                hi(None, wh[cc][:, :], (up_done, 3 + cc, cc, 16 * (P_UP // 2 + 2)))
            for cc in range(2):
                hi(None, wdh[:, cc, :], (None, None, cc, 16 * (P_UP // 2 + 3)))
            with act.Fori(0, (GROUPS - 2) // 2) as i:
                for par in range(2):
                    act_group(2 * i + par + 1, 1 - par, True, True)
            act_group(GROUPS - 1, (GROUPS - 1) % 2, False, True)
            act.wait_ge(w_lo, PIECES)
            for n, tiles in enumerate(final):
                for t in tiles:
                    act.wait_ge(y_added, 8 * (GROUPS - 1) + t + 1)
                    if t >= 1:
                        act.wait_ge(fin_sq, t)
                    act.activation(out_junk[:, :], yacc[t // 4][:, t % 4, :], ACT.Square,
                                   accum_out=mean_sq[:, 3, t:t + 1]).then_inc(fin_sq, 1)
                ts = slice(tiles[0], tiles[-1] + 1)
                act.wait_ge(fin_var, n + 1)
                act.activation(root[:, ts], var[:, ts], ACT.Sqrt).then_inc(fin_root, 1)

        @block.vector
        def _(dve):
            chain = [0]

            def link(ins):
                chain[0] += 1
                ins.then_inc(dve_chain, 1)
                dve.wait_ge(dve_chain, chain[0])

            def lo(dst, src_hi, s, n):
                dve.wait_ge(w_hi, n)
                dve.tensor_tensor(dst, raw[s][:, :], src_hi.bitcast(F32), ALU.subtract).then_inc(w_lo, 1)

            def lo_early(p):
                lo(wl[p % 2][:, :], wh[p % 2][:, :], p % 2, p + 1)

            def rsqrt_pre(sums, v, n, signal):
                dve.tensor_scalar(v, sums, 1.0 / n, EPS, ALU.mult, ALU.add).then_inc(signal, 1)

            def rsqrt_post(v, r, a, b, result, signal=None):
                link(dve.reciprocal(a, r))
                link(dve.tensor_tensor(b, v, a, ALU.mult))
                link(dve.scalar_tensor_tensor(b, b, -0.5, a, ALU.mult, ALU.mult))
                ins = dve.scalar_tensor_tensor(result, b, 1.5, a, ALU.add, ALU.mult)
                ins.then_inc(signal, 1) if signal else link(ins)

            dve.memset(ones[:, :], 1.0).then_inc(const_ready, 1)
            for gq in range(2):
                sl = slice(4 * gq, 4 * gq + 4)
                dve.wait_ge(x_loaded[2 * gq + 1], 16)
                t = 4 * gq + 3
                dve.tensor_tensor_reduce(out=u_t[:, 2 + gq, :], in0=x_sb[:, t, :], in1=x_sb[:, t, :], scale=1.0,
                                         scalar=0.0, op0=ALU.mult, op1=ALU.add,
                                         accum_out=mean_sq[:, 0, t:t + 1]).then_inc(squares_v, 1)
                dve.wait_ge(squares_v, gq + 1)
                dve.wait_ge(squares, 3 * gq + 3)
                rsqrt_pre(mean_sq[:, 0, sl], var[:, sl], D, var_ready)
                dve.wait_ge(root_ready, gq + 1)
                rsqrt_post(var[:, sl], root[:, sl], t1[:, sl], t2[:, sl], rstd[:, 0, sl])
                for t in range(4 * gq, 4 * gq + 4):
                    dve.tensor_scalar(x_sb[:, t, :], x_sb[:, t, :], rstd[:, 0, t:t + 1], None,
                                      ALU.mult).then_inc(scaled, 1)

            def split_lo(n, dst_h, dst_l, gain0, b):
                hf, k = divmod(n % 16, KC)
                cols_ = slice(HALF * hf, HALF * hf + HALF)
                dve.wait_ge(tr_hi, n + 1)
                dve.scalar_tensor_tensor(dst_l[:, k, cols_], bank(b), cols[:, gain0 + k:gain0 + k + 1],
                                         dst_h[:, k, cols_].bitcast(F32), ALU.mult,
                                         ALU.subtract).then_inc(tr_lo, 1)

            lo_early(0)
            dve.wait_ge(ident_loaded, 32)
            for n in range(2 * KC):
                split_lo(n, xh, xl, C_GPRE, n % KC)
            lo_early(1)
            dve.wait_ge(small_loaded, 32)
            link(dve.tensor_scalar(head_gain[:, :], cols[:, C_HEADG:C_HEADG + 1], 1.0 - LAM_INIT, None, ALU.mult))
            link(dve.tensor_scalar(tiny[:, 2, :], cols[:, C_LAM:C_LAM + LC], -1.0, None, ALU.mult))
            link(dve.tensor_tensor(tiny[:, 0, :], tiny[:, 2, :], cols[:, C_LAM:C_LAM + LC], ALU.max))
            for m in range(2):
                link(dve.tensor_tensor(lam_raw[:, 2 * m, :], lam_raw[:, 2 * m, :], lam_raw[:, 2 * m + 1, :], ALU.mult))
                link(dve.tensor_reduce(lam_e[:, m:m + 1], lam_raw[:, 2 * m, :], AX.X, ALU.add))
            dve.tensor_scalar(tiny[:, 2, :], tiny[:, 2, :], 0.0, None, ALU.max).then_inc(lam_step, 1)
            dve.wait_ge(act_step, 2)
            dve.wait_ge(lam_step, 1)
            link(dve.tensor_tensor(lam_e[:, 0:1], lam_e[:, 2:3], lam_e[:, 3:4], ALU.subtract))
            link(dve.tensor_scalar(lam_e[:, 1:2], lam_e[:, 0:1], -1.0, -LAM_INIT, ALU.mult, ALU.add))
            e_, z_, z2, acc = tiny[:, 1, :], tiny[:, 3, :], tiny[:, 4, :], tiny[:, 5, :]
            link(dve.tensor_scalar(z_, e_, 2.0, None, ALU.add))
            link(dve.reciprocal(acc, z_))
            link(dve.tensor_tensor(z_, e_, acc, ALU.mult))
            link(dve.tensor_tensor(z2, z_, z_, ALU.mult))
            link(dve.tensor_scalar(acc, z2, 1.0 / 17, 1.0 / 15, ALU.mult, ALU.add))
            for n in (13, 11, 9, 7, 5, 3, 1):
                link(dve.tensor_tensor(acc, acc, z2, ALU.mult))
                link(dve.tensor_scalar(acc, acc, 1.0 / n, None, ALU.add))
            link(dve.tensor_tensor(acc, acc, z_, ALU.mult))
            link(dve.scalar_tensor_tensor(acc, acc, 2.0, tiny[:, 2, :], ALU.mult, ALU.add))
            link(dve.tensor_scalar(spl[:, 0, :], acc, LRU_C, None, ALU.mult))
            dve.tensor_scalar(spl[:, 1, :], acc, -LRU_C, None, ALU.mult).then_inc(dve_step, 1)
            with dve.Fori(0, LC) as c:
                dve.wait_ge(lru_copied, 2 * c + 1)
                for tap in range(TAPS):
                    k = TAPS - 1 - tap
                    w_col = cols[:, bass.ds(c + C_CONVW + LC * k, 1)]
                    if tap == 0:
                        ins = dve.tensor_scalar(xc_t[:, c, :], u_t[:, c, :], w_col,
                                                cols[:, bass.ds(c + C_CONVB, 1)], ALU.mult, ALU.add)
                    else:
                        ins = dve.scalar_tensor_tensor(xc_t[:, c, tap:T], u_t[:, c, 0:T - tap], w_col,
                                                       xc_t[:, c, tap:T], ALU.mult, ALU.add)
                    if tap < TAPS - 1:
                        ins.then_inc(conv_step, 1)
                        dve.wait_ge(conv_step, 3 * c + tap + 1)
                    else:
                        ins.then_inc(conv_done, 1)
                lo(wl[0][:, :], wh[0][:, :], 0, 2 * c + 3)
                dve.wait_ge(xc_hi, c + 1)
                dve.tensor_tensor(gwl[:, :, :], gw_raw[:, c, :, :], gwh[:, :, :].bitcast(F32), ALU.subtract)
                dve.wait_ge(conv_done, c + 1)
                dve.tensor_tensor(xcl[:, :], xc_t[:, c, :], xch[:, :].bitcast(F32), ALU.subtract).then_inc(xc_lo, 1)
                dve.wait_ge(gelu_sq, c + 1)
                dve.tensor_scalar(lru_g[:, :], lru_g[:, :], GELU_A, 1.0, ALU.mult, ALU.add).then_inc(gelu_step, 1)
                dve.wait_ge(gelu_step, c + 1)
                dve.tensor_tensor(lru_g[:, :], lru_g[:, :], gel[:, c, :], ALU.mult).then_inc(gelu_in, 1)
                lo(wl[1][:, :], wh[1][:, :], 1, 2 * c + 4)
                dve.wait_ge(sig_done, 2 * c + 2)
                dve.tensor_tensor(xc_t[:, c, :], xc_t[:, c, :], lru_a[:, :], ALU.mult).then_inc(ix_done, 1)
                dve.wait_ge(gelu_sig, c + 1)
                dve.tensor_tensor(gel[:, c, :], gel[:, c, :], lru_g[:, :], ALU.mult).then_inc(gelu_done, 1)
            for c in range(LC):
                dve.wait_ge(decay_sq, c + 1)
                dve.wait_ge(tanh_done, LC)
                dve.scalar_tensor_tensor(u_t[:, c, :], lru_a[:, :], 1.0, u_t[:, c, :], ALU.add,
                                         ALU.mult).then_inc(bsq_done, 1)
                if c == 1:
                    lo_early(P_VA + 2)
            for c in range(LC):
                dve.wait_ge(sqrt_done, c + 1)
                dve.wait_ge(ix_done, LC)
                dve.tensor_tensor(xc_t[:, c, :], xc_t[:, c, :], u_t[:, c, :], ALU.mult).then_inc(scan_step, 1)
                dve.wait_ge(scan_step, 2 * c + 1)
                dve.tensor_tensor_scan(u_t[:, c, :], dec[:, c, :], xc_t[:, c, :], 0.0, ALU.mult,
                                       ALU.add).then_inc(scan_step, 1)
                dve.wait_ge(scan_step, 2 * c + 2)
                dve.wait_ge(gelu_done, LC)
                dve.tensor_tensor(gel[:, c, :], u_t[:, c, :], gel[:, c, :], ALU.mult).then_inc(lru_done, 1)
                if c == 0:
                    lo_early(P_VA + 3)
                if c == 2:
                    lo_early(P_QK)

            def v_lows(half):
                for t in range(4 * half, 4 * half + 4):
                    dve.wait_ge(v_hi, t + 1)
                    dve.tensor_tensor(vl[:, t, :], bank(4 + t % 4), vh[:, t, :].bitcast(F32),
                                      ALU.subtract).then_inc(v_lo, 1)

            v_lows(0)
            lo_early(P_QK + 1)
            dve.wait_ge(rope_loaded, 16)
            with dve.Fori(0, HEADS) as h:
                for s in range(2):
                    lo(wl[s][:, :], wh[s][:, :], s, 2 * h + P_QK + s + 3)
                    dve.wait_ge(q_copied, 2 * h + s + 1)
                    dve.wait_ge(rot_loaded, 128 * h + 64 * (s + 1))
                    dve.tensor_tensor(q_sb[:, s, :], q_sb[:, s, :], cos_t[:, 0, :], ALU.mult).then_inc(rope_step, 1)
                    dve.tensor_tensor(q_rot[:, :], q_rot[:, :], cos_t[:, 1, :], ALU.mult).then_inc(rope_step, 1)
                    dve.wait_ge(rope_step, 4 * h + 2 * s + 2)
                    dve.tensor_tensor(q_sb[:, s, :], q_sb[:, s, :], q_rot[:, :], ALU.add).then_inc(rope_sum, 1)
                    dve.wait_ge(rope_sum, 2 * h + s + 1)
                    dve.wait_ge(qk_hi, 2 * h + s + 1)
                    dve.scalar_tensor_tensor(yl[:, 2 * h + s, :], q_sb[:, s, :], Q_SCALE if s == 0 else 1.0,
                                             yh[:, 2 * h + s, :].bitcast(F32), ALU.mult,
                                             ALU.subtract).then_inc(qk_lo, 1)
            lo_early(P_VB + 2)
            lo_early(P_VB + 3)
            lo_early(P_OUT)
            v_lows(1)
            steps = TT * HEADS
            seen = [0]

            def combine_step(p):
                keys = slice(0, P * (p % TT + 1))
                dve.wait_ge(exped, 2 * p + 2)
                c = blend[:, p % 2:p % 2 + 1]
                link(dve.reciprocal(c, sum1[:, p % 2:p % 2 + 1]))
                link(dve.scalar_tensor_tensor(c, c, sum0[:, p:p + 1], lam_e[:, 1:2], ALU.mult, ALU.mult))
                dve.scalar_tensor_tensor(probs[:, p % 2, 0, keys], probs[:, p % 2, 1, keys], c,
                                         probs[:, p % 2, 0, keys], ALU.mult, ALU.add).then_inc(w_done, 1)

            def max_step(s):
                for m in range(2):
                    dve.wait_ge(scores, 2 * s + m + 1)
                    dve.tensor_reduce(negmax[:, s % 2, m:m + 1], score_bank(s, m)[:, 0:P * (s % TT + 1)], AX.X, ALU.max,
                                      negate=True).then_inc(maxed, 1)

            def wt_lo_step(p):
                i, j = p % TT, p // 2
                th, tl = (xl[:, 0:2, :], xl[:, 2:4, :]) if j % 2 == 0 else (wt2h, wt2l)
                if j % 2 == 0:
                    th = th.rearrange("p a (b q) -> p (a b) q", q=2 * P)
                    tl = tl.rearrange("p a (b q) -> p (a b) q", q=2 * P)
                for b in range(i // 4 + 1):
                    dve.wait_ge(wt_hi, seen[0] + 1)
                    nb = min(4, i + 1 - 4 * b)
                    kq = (slice(None), slice(4 * b, 4 * b + nb), slice(P * (p % 2), P * (p % 2) + P))
                    dve.tensor_tensor(tl[kq], bank(w_banks[seen[0] % 3])[:, 0:P * nb].rearrange("p (k q) -> p k q", q=P),
                                      th[kq].bitcast(F32), ALU.subtract).then_inc(wt_lo, 1)
                    seen[0] += 1

            for s in range(steps + 2):
                max_first = s < steps and s % TT < TT // 2 and s % 2 == 0
                if max_first:
                    max_step(s)
                if 1 <= s <= steps:
                    combine_step(s - 1)
                if s < steps and not max_first:
                    max_step(s)
                if s >= 2:
                    wt_lo_step(s - 2)
                if s == 5:
                    lo_early(P_OUT + 1)
            link(dve.tensor_tensor(sum0_eps[:, :], sum0[:, :], sum0[:, :], ALU.mult))
            link(dve.tensor_scalar(sum0_eps[:, :], sum0_eps[:, :], EPS, None, ALU.mult))
            dve.wait_ge(sumsq_done, steps // 2)
            dve.scalar_tensor_tensor(hvar[:, :], head_sums, 1.0 / P, sum0_eps[:, :], ALU.mult,
                                     ALU.add).then_inc(head_var, 1)
            dve.wait_ge(head_root, 1)
            rsqrt_post(hvar[:, :], hroot[:, :], ht1[:, :], ht2[:, :], hrstd[:, :])

            def diagonals(h):
                if h >= 2:
                    dve.wait_ge(spread_done, 2 * (h - 1))
                for t in range(TT):
                    ins = dve.tensor_scalar(diag[:, h % 2, P * t:P * t + P], ident[:, :],
                                            hrstd[:, TT * h + t:TT * h + t + 1], None, ALU.mult)
                ins.then_inc(diag_done, 1)

            for h in range(0, HEADS, 2):
                diagonals(h)
                diagonals(h + 1)
                lo_early(P_OUT + 2 + h // 2)
                for n in range(h, h + 2):
                    dve.wait_ge(spread_done, 2 * n + 2)
                    dve.scalar_tensor_tensor(o_raw[:, 2 * n, :], o_raw[:, 2 * n, :], head_gain[:, 0:1],
                                             pair[2 + n % 2][:, :], ALU.mult, ALU.mult).then_inc(o_norm, 1)
                for n in range(h, h + 2):
                    dve.wait_ge(o_norm, n + 1)
                    dve.wait_ge(mix_hi, LC + n + 1)
                    dve.tensor_tensor(xl[:, n, :], o_raw[:, 2 * n, :], xh[:, n, :].bitcast(F32),
                                      ALU.subtract).then_inc(mix_lo, 1)

            def post_mean(half):
                sl = slice(4 * half, 4 * half + 4)
                dve.wait_ge(y_copied, 8 * half + 8)
                link(dve.tensor_tensor(mean_sq[:, 1, sl], mean_sq[:, 1, sl], mean_sq[:, 4, sl], ALU.add))
                rsqrt_pre(mean_sq[:, 1, sl], var[:, sl], D, post_var)

            def post_norm(half):
                sl = slice(4 * half, 4 * half + 4)
                dve.wait_ge(post_root, half + 1)
                rsqrt_post(var[:, sl], root[:, sl], t1[:, sl], t2[:, sl], rstd[:, 1, sl])

            def y_scale(half, tiles):
                for n in tiles:
                    t = 4 * half + n
                    dve.scalar_tensor_tensor(h_sb[:, t, :], h_sb[:, t, :], rstd[:, 1, t:t + 1], g_post[:, :],
                                             ALU.mult, ALU.mult).then_inc(y_scaled, 1)

            def x_add(half):
                dve.wait_ge(x_back, 16 * (4 + half))
                for n in range(2, 4):
                    t = 4 * half + n
                    dve.wait_ge(y_scaled, t + 1)
                    hv = halves(h_sb[:, t, :])
                    xv = halves(x_b[:, n, :]) if half else tile_a(x_a, n)
                    dve.tensor_tensor(hv, hv, xv, ALU.add).then_inc(h_done, 1)

            def pre_norm(half):
                sl = slice(4 * half, 4 * half + 4)
                dve.wait_ge(h_squared, 4 * half + 4)
                rsqrt_pre(mean_sq[:, 2, sl], var[:, sl], D, pre_var)
                dve.wait_ge(pre_root, half + 1)
                rsqrt_post(var[:, sl], root[:, sl], t1[:, sl], t2[:, sl], rstd[:, 2, sl], pre_rstd)
                if half == 1:
                    dve.wait_ge(pre_rstd, 2)
                    for t in range(2, 4):
                        dve.tensor_scalar(hm_b[:, t, :], h_sb[:, 4 + t, :], rstd[:, 2, 4 + t:5 + t], None,
                                          ALU.mult).then_inc(hm_scaled_v, 1)

            for quarter in range(2):
                for j in range(4 if quarter == 0 else 2, 6):
                    lo_early(P_OUT + 4 * quarter + j)
            dve.wait_ge(g_post_loaded, 16)
            p = P_OUT + 8
            post_mean(0)
            lo_early(p + 2)
            post_norm(0)
            y_scale(0, (0, 1))
            lo_early(p + 3)
            y_scale(0, (2, 3))
            x_add(0)
            lo_early(p + 4)
            pre_norm(0)
            lo_early(p + 5)
            p = P_OUT + 12
            lo_early(p + 2)
            for k in range(4):
                split_lo(16 + k, yh, yl, C_GMLP, k)
            lo_early(p + 3)
            for k in range(4, KC):
                split_lo(16 + k, yh, yl, C_GMLP, k % 4)
            lo_early(p + 4)
            post_mean(1)
            post_norm(1)
            y_scale(1, range(4))
            x_add(1)
            lo_early(p + 5)
            pre_norm(1)
            for k in range(KC):
                split_lo(24 + k, yh, yl, C_GMLP, 4 + k % 4)

            def act_unit(g, par, cc, hf):
                first = isinstance(g, int) and g == 0
                n, slot = (2 * hf + cc, cc) if first else (4 * g + 2 * cc + hf, hf)
                dve.wait_ge(act_hi, n + 1)
                dve.tensor_tensor(relu[:, slot, :], relu[:, slot, :], relu[:, slot, :],
                                  ALU.mult).then_inc(relu_sq, 1)
                dve.wait_ge(relu_sq, n + 1)
                tok = slice(HALF * hf, HALF * hf + HALF)
                dve.tensor_tensor(xl[:, 2 * par + cc, tok], relu[:, slot, :], xh[:, 2 * par + cc, tok].bitcast(F32),
                                  ALU.subtract).then_inc(act_lo, 1)

            def sums(g):
                for t in range(TT):
                    dve.wait_ge(down_done, 8 * g + t + 1)
                    y = yacc[t // 4][:, t % 4, :]
                    dve.tensor_tensor(y, y, pair[2 + t % 2][:, :], ALU.add).then_inc(y_added, 1)

            def act_group(g, par, up_next):
                for cc in range(2):
                    act_unit(g, par, cc, 0)
                    act_unit(g, par, cc, 1)
                    if up_next:
                        lo(wl[cc][:, :], wh[cc][:, :], cc, 4 * g + P_UP + 2 + cc + 1)

            def down_lo(g, up_next):
                for cc in range(2):
                    lo(wdl[:, cc, :], wdh[:, cc, :], cc, 4 * g + P_UP + (4 if up_next else 2) + cc + 1)

            for hf in range(2):
                for cc in range(2):
                    act_unit(0, 0, cc, hf)
            for cc in range(2):
                lo(wl[cc][:, :], wh[cc][:, :], cc, P_UP + 2 + cc + 1)
            down_lo(0, True)
            dve.wait_ge(acc_zero, 2)
            with dve.Fori(0, (GROUPS - 2) // 2) as i:
                for par in range(2):
                    g = 2 * i + par + 1
                    act_group(g, 1 - par, True)
                    sums(g - 1)
                    down_lo(g, True)
            act_group(GROUPS - 1, (GROUPS - 1) % 2, False)
            sums(GROUPS - 2)
            down_lo(GROUPS - 1, False)
            dve.wait_ge(g_out_loaded, 16)

            def finish(n):
                tiles = final[n]
                ts = slice(tiles[0], tiles[-1] + 1)
                dve.wait_ge(fin_sq, tiles[-1] + 1)
                rsqrt_pre(mean_sq[:, 3, ts], var[:, ts], D, fin_var)
                dve.wait_ge(fin_root, n + 1)
                rsqrt_post(var[:, ts], root[:, ts], t1[:, ts], t2[:, ts], rstd[:, 3, ts])
                for t in tiles:
                    y = yacc[t // 4][:, t % 4, :]
                    dve.scalar_tensor_tensor(y, y, rstd[:, 3, t:t + 1], g_out[:, :], ALU.mult,
                                             ALU.mult).then_inc(fin_scaled, 1)

            for n, tiles in enumerate(final):
                for t in tiles:
                    dve.wait_ge(down_done, 8 * (GROUPS - 1) + t + 1)
                    y = yacc[t // 4][:, t % 4, :]
                    dve.tensor_tensor(y, y, pair[last_pair(t)][:, :], ALU.add).then_inc(y_added, 1)
                if n >= 1:
                    finish(n - 1)
            finish(len(final) - 1)


def row_pieces(w, n_cols):
    r = D // n_cols
    w = w.reshape(-1, r, P, w.shape[1] // n_cols, n_cols)
    return w.transpose(3, 0, 2, 1, 4).reshape(-1, P, D)


def column_pieces(w):
    return w.reshape(KC, P, -1, P).transpose(2, 1, 0, 3).reshape(-1, P, D)


def lay_out_weights(w_in, w_out, w_up, w_down):
    u, g = column_pieces(w_in[:, :LRU]), column_pieces(w_in[:, LRU:2 * LRU])
    q = column_pieces(w_in[:, 2 * LRU:2 * LRU + HALF])
    k = column_pieces(w_in[:, 2 * LRU + HALF:2 * LRU + 2 * HALF])
    v = row_pieces(w_in[:, 2 * LRU + 2 * HALF:], HALF)
    up = column_pieces(w_up).reshape(GROUPS, 2, P, D)
    down = w_down.reshape(GROUPS, 2, P, D)
    parts = [np.stack([u, g], 1).reshape(-1, P, D), v, np.stack([q, k], 1).reshape(-1, P, D), v,
             row_pieces(w_out, HALF), row_pieces(w_out, HALF), up[0]]
    for n in range(GROUPS):
        if n + 1 < GROUPS:
            parts.append(up[n + 1])
        parts.append(down[n])
    return np.concatenate(parts)


def lay_out_gates(wa, wx):
    g = np.zeros((P, LC, 2, P), np.float32)
    for n, w in enumerate((wa, wx)):
        for c in range(LC):
            for b in range(2):
                g[64 * b:64 * b + 64, c, n, 64 * b:64 * b + 64] = w[2 * c + b]
    return g


def lay_out_columns(i):
    def col(v):
        return np.asarray(v).reshape(-1, P).T
    c = [col(i["norm_mix_pre"][0]), col(i["norm_mlp_pre"][0])]
    c += [col(i["conv_w"][0][k]) for k in range(TAPS)]
    c += [col(i["conv_b"][0]), col(i["b_gate_a"][0]), col(i["b_gate_x"][0]), col(i["lru_lambda"][0]),
          col(i["att_head_norm"][0])]
    return np.ascontiguousarray(np.concatenate(c, 1))


def rope_tables():
    half = np.float32(32)
    freqs = np.float32(10000.0) ** (-np.arange(32, dtype=np.float32) / half)
    ang = np.arange(T, dtype=np.float32)[:, None] * freqs[None, :]
    cos, sin = np.cos(ang).T, np.sin(ang).T
    return np.stack([np.concatenate([cos] * 4), np.concatenate([-sin, sin] * 2)], 1).astype(np.float32)


def kernel(**inputs):
    import concourse.bacc as bacc
    from concourse.bass_utils import run_bass_kernel_spmd

    i = {n: np.asarray(a) for n, a in inputs.items()}
    mask = np.where(np.arange(P)[None, :] > np.arange(P)[:, None], MASKED, 0.0)
    arrays = {
        "x": i["x"],
        "weights": lay_out_weights(i["w_in"][0], i["w_out"][0], i["w_up"][0], i["w_down"][0]),
        "gate_weights": lay_out_gates(i["w_gate_a"][0], i["w_gate_x"][0]),
        "columns": lay_out_columns(i),
        "lam_rows": np.stack([i[n][0] for n in ("lambda_q1", "lambda_k1", "lambda_q2", "lambda_k2")]),
        "post_gains": np.stack([i["norm_mix_post"][0], i["norm_mlp_post"][0]]),
        "rope": rope_tables(),
        "constants": np.stack([np.eye(P), mask]).astype(np.float32),
    }
    arrays = {n: np.ascontiguousarray(a) for n, a in arrays.items()}
    nc = bacc.Bacc("TRN2", target_bir_lowering=False, num_devices=1)
    args = [nc.dram_tensor(n, a.shape, mybir.dt.from_np(a.dtype), kind="ExternalInput").ap()
            for n, a in arrays.items()]
    spill = nc.dram_tensor("y_spill", (LC, P, T), F32, kind="Internal").ap()
    out = nc.dram_tensor("out", (1, T, D), F32, kind="ExternalOutput").ap()
    build(nc, *args, spill, out)
    return run_bass_kernel_spmd(nc, [arrays], core_ids=[0]).results[0]["out"]
```
